# Optimizing a Trainium2 kernel written in Bass

```python
import math
import jax, jax.numpy as jnp
from jax import lax
import numpy as np

D_MODEL = 1024
BATCH = 1
SEQ = 512
DEPTH = 2

CHUNK = 64
D_MIX = D_MODEL
CONV_CH = D_MIX // 4
CONV_WIDTH = 31
HEAD_DIM = 64
N_Q_HEADS = (D_MIX // 2) // HEAD_DIM
N_KV_HEADS = 2
Q_PER_KV = N_Q_HEADS // N_KV_HEADS
ATTN_WIDTH = N_Q_HEADS * HEAD_DIM
KV_WIDTH = N_KV_HEADS * HEAD_DIM
WINDOW = 128
WINDOW_CHUNKS = WINDOW // CHUNK
ROPE_THETA = 500000.0
ROPE_DIM = HEAD_DIM // 4
GMLP_WIDTH = D_MIX // 4
GMLP_HEADS = 4
GMLP_HEAD_DIM = GMLP_WIDTH // GMLP_HEADS
GMLP_BLOCK = 128
OFF_CONV = 0
OFF_Q = OFF_CONV + 2 * CONV_CH
OFF_K = OFF_Q + ATTN_WIDTH
OFF_V = OFF_K + KV_WIDTH
OFF_GMLP = OFF_V + KV_WIDTH
D_IN = OFF_GMLP + 2 * GMLP_WIDTH
N_EXPERTS = 16
N_GROUPS = 4
EXPERTS_PER_GROUP = N_EXPERTS // N_GROUPS
TOP_K = 2
D_EXPERT = D_MODEL // 2
LN_EPS = 1e-5
DN_ALPHA = (2 * DEPTH) ** 0.25
DN_BETA = (8 * DEPTH) ** -0.25

kernel_name = 'hybrid_conv_swa_gmlp_moe_block'

def layer_norm(x, g, b):
    xf = x.astype(jnp.float32)
    mu = jnp.mean(xf, axis=-1, keepdims=True)
    var = jnp.mean(jnp.square(xf - mu), axis=-1, keepdims=True)
    y = (xf - mu) * lax.rsqrt(var + LN_EPS)
    return (y * g.astype(jnp.float32) + b.astype(jnp.float32)).astype(x.dtype)

def causal_depthwise_conv(h, w, b):
    c = h.shape[-1]
    hp = jnp.pad(h, ((0, 0), (CONV_WIDTH - 1, 0), (0, 0)))
    y = lax.conv_general_dilated(hp, w[:, None, :], window_strides=(1,), padding='VALID',
                                 dimension_numbers=('NWC', 'WIO', 'NWC'), feature_group_count=c)
    return y + b

def partial_rotary(x, pos):
    half = ROPE_DIM // 2
    inv_freq = jnp.power(ROPE_THETA, -jnp.arange(half, dtype=jnp.float32) / half)
    ang = pos[:, None] * inv_freq[None, :]
    cos = jnp.cos(ang)[None, :, None, :].astype(x.dtype)
    sin = jnp.sin(ang)[None, :, None, :].astype(x.dtype)
    x1 = x[..., :half]
    x2 = x[..., half:ROPE_DIM]
    return jnp.concatenate([x1 * cos - x2 * sin, x2 * cos + x1 * sin, x[..., ROPE_DIM:]], axis=-1)

def chunk_band(t):
    n_c = t.shape[1]
    tp = jnp.pad(t, ((0, 0), (WINDOW_CHUNKS - 1, 0), (0, 0), (0, 0), (0, 0)))
    return jnp.concatenate([tp[:, s:s + n_c] for s in range(WINDOW_CHUNKS)], axis=2)

def sliding_window_sink_attention(q, k, v, sinks):
    bsz, t = q.shape[:2]
    n_c = t // CHUNK
    qc = q.reshape(bsz, n_c, CHUNK, N_KV_HEADS, Q_PER_KV, HEAD_DIM)
    kb = chunk_band(k.reshape(bsz, n_c, CHUNK, N_KV_HEADS, HEAD_DIM))
    vb = chunk_band(v.reshape(bsz, n_c, CHUNK, N_KV_HEADS, HEAD_DIM))
    s = jnp.einsum('bcqgrd,bckgd->bgrcqk', qc, kb).astype(jnp.float32) * (HEAD_DIM ** -0.5)
    chunk_idx = jnp.arange(n_c)[:, None]
    key_block = jnp.arange(WINDOW_CHUNKS * CHUNK)[None, :] // CHUNK
    valid = (chunk_idx + key_block - (WINDOW_CHUNKS - 1)) >= 0
    s = jnp.where(valid[None, None, None, :, None, :], s, -1e30)
    sink = jnp.broadcast_to(sinks.astype(jnp.float32).reshape(1, N_KV_HEADS, Q_PER_KV, 1, 1, 1),
                            s.shape[:-1] + (1,))
    p = jax.nn.softmax(jnp.concatenate([s, sink], axis=-1), axis=-1)[..., :-1].astype(v.dtype)
    o = jnp.einsum('bgrcqk,bckgd->bcqgrd', p, vb)
    return o.reshape(bsz, t, ATTN_WIDTH)

def spatial_gating(z, ln_g, ln_b, w_s, b_s):
    bsz, t = z.shape[:2]
    u = z[..., :GMLP_WIDTH]
    v = layer_norm(z[..., GMLP_WIDTH:], ln_g, ln_b)
    n_s = t // GMLP_BLOCK
    vs = v.reshape(bsz, n_s, GMLP_BLOCK, GMLP_HEADS, GMLP_HEAD_DIM)
    blk = jnp.arange(GMLP_BLOCK) // CHUNK
    mask = blk[None, :] <= blk[:, None]
    w = jnp.where(mask[None], w_s, 0.0)
    sv = jnp.einsum('hij,bsjhc->bsihc', w, vs) + b_s.T[None, None, :, :, None]
    return u * sv.reshape(bsz, t, GMLP_WIDTH)

def mixing_sublayer(x, pos, w_in, b_in, conv_w, conv_b, conv_ln_g, conv_ln_b, sinks,
                    gmlp_ln_g, gmlp_ln_b, gmlp_w_s, gmlp_b_s, w_out, b_out):
    bsz, t, _ = x.shape
    h = x @ w_in + b_in
    a = h[..., OFF_CONV:OFF_CONV + CONV_CH]
    g = h[..., OFF_CONV + CONV_CH:OFF_Q]
    c = causal_depthwise_conv(a * jax.nn.sigmoid(g), conv_w, conv_b)
    c = jax.nn.silu(layer_norm(c, conv_ln_g, conv_ln_b))
    q = partial_rotary(h[..., OFF_Q:OFF_K].reshape(bsz, t, N_Q_HEADS, HEAD_DIM), pos)
    k = partial_rotary(h[..., OFF_K:OFF_V].reshape(bsz, t, N_KV_HEADS, HEAD_DIM), pos)
    v = h[..., OFF_V:OFF_GMLP].reshape(bsz, t, N_KV_HEADS, HEAD_DIM)
    att = sliding_window_sink_attention(q, k, v, sinks)
    gm = spatial_gating(jax.nn.gelu(h[..., OFF_GMLP:]), gmlp_ln_g, gmlp_ln_b, gmlp_w_s, gmlp_b_s)
    cat = jnp.concatenate([c, att, gm], axis=-1)
    return cat @ w_out + b_out

def group_limited_router(x2d, w_router, router_bias):
    n = x2d.shape[0]
    logits = x2d.astype(jnp.float32) @ w_router.astype(jnp.float32)
    scores = jax.nn.softmax(logits, axis=-1)
    sel = scores + router_bias.astype(jnp.float32)
    sel_g = sel.reshape(n, N_GROUPS, EXPERTS_PER_GROUP)
    group_score = jnp.sum(lax.top_k(sel_g, TOP_K)[0], axis=-1)
    best = jnp.argmax(group_score, axis=-1)
    in_group = jnp.arange(N_GROUPS)[None, :] == best[:, None]
    masked = jnp.where(in_group[:, :, None], sel_g, -jnp.inf).reshape(n, N_EXPERTS)
    _, idx = lax.top_k(masked, TOP_K)
    wts = jnp.take_along_axis(scores, idx, axis=-1)
    wts = wts / jnp.sum(wts, axis=-1, keepdims=True)
    return jnp.sum(jax.nn.one_hot(idx, N_EXPERTS, dtype=jnp.float32) * wts[..., None], axis=-2)

def moe_ffn(x, w_router, router_bias, w_gate, w_up, w_down):
    bsz, t, d = x.shape
    x2d = x.reshape(bsz * t, d)
    gates = group_limited_router(x2d, w_router, router_bias)
    y = jnp.zeros((bsz * t, d), jnp.float32)
    for e in range(N_EXPERTS):
        he = jax.nn.silu(x2d @ w_gate[e]) * (x2d @ w_up[e])
        y = y + gates[:, e:e + 1] * (he @ w_down[e]).astype(jnp.float32)
    return y.astype(x.dtype).reshape(bsz, t, d)

def setup_inputs(seed: int = 0) -> dict:
    key = jax.random.key(seed)
    ks = jax.random.split(key, 24)
    f32 = jnp.float32

    def nrm(k, shape, scale):
        return jax.random.normal(k, shape, f32) * scale

    return {
        'x': nrm(ks[0], (BATCH, SEQ, D_MODEL), 1.0),
        'w_in': nrm(ks[1], (DEPTH, D_MODEL, D_IN), D_MODEL ** -0.5),
        'b_in': nrm(ks[2], (DEPTH, D_IN), 0.02),
        'conv_w': nrm(ks[3], (DEPTH, CONV_WIDTH, CONV_CH), CONV_WIDTH ** -0.5),
        'conv_b': nrm(ks[4], (DEPTH, CONV_CH), 0.02),
        'conv_ln_g': 1.0 + nrm(ks[5], (DEPTH, CONV_CH), 0.02),
        'conv_ln_b': nrm(ks[6], (DEPTH, CONV_CH), 0.02),
        'attn_sinks': nrm(ks[7], (DEPTH, N_Q_HEADS), 0.5),
        'gmlp_ln_g': 1.0 + nrm(ks[8], (DEPTH, GMLP_WIDTH), 0.02),
        'gmlp_ln_b': nrm(ks[9], (DEPTH, GMLP_WIDTH), 0.02),
        'gmlp_w_s': nrm(ks[10], (DEPTH, GMLP_HEADS, GMLP_BLOCK, GMLP_BLOCK), GMLP_BLOCK ** -0.5),
        'gmlp_b_s': 1.0 + nrm(ks[11], (DEPTH, GMLP_HEADS, GMLP_BLOCK), 0.02),
        'w_out': nrm(ks[12], (DEPTH, D_MIX, D_MODEL), (D_MIX ** -0.5) * DN_BETA),
        'b_out': nrm(ks[13], (DEPTH, D_MODEL), 0.02),
        'ln_mix_g': 1.0 + nrm(ks[14], (DEPTH, D_MODEL), 0.02),
        'ln_mix_b': nrm(ks[15], (DEPTH, D_MODEL), 0.02),
        'w_router': nrm(ks[16], (D_MODEL, N_EXPERTS), D_MODEL ** -0.5),
        'router_bias': nrm(ks[17], (N_EXPERTS,), 0.01),
        'exp_w_gate': nrm(ks[18], (DEPTH, N_EXPERTS, D_MODEL, D_EXPERT), D_MODEL ** -0.5),
        'exp_w_up': nrm(ks[19], (DEPTH, N_EXPERTS, D_MODEL, D_EXPERT), D_MODEL ** -0.5),
        'exp_w_down': nrm(ks[20], (DEPTH, N_EXPERTS, D_EXPERT, D_MODEL), (D_EXPERT ** -0.5) * DN_BETA),
        'ln_ffn_g': 1.0 + nrm(ks[21], (DEPTH, D_MODEL), 0.02),
        'ln_ffn_b': nrm(ks[22], (DEPTH, D_MODEL), 0.02),
    }

def reference(x, w_in, b_in, conv_w, conv_b, conv_ln_g, conv_ln_b, attn_sinks,
              gmlp_ln_g, gmlp_ln_b, gmlp_w_s, gmlp_b_s, w_out, b_out, ln_mix_g, ln_mix_b,
              w_router, router_bias, exp_w_gate, exp_w_up, exp_w_down, ln_ffn_g, ln_ffn_b):
    pos = jnp.arange(x.shape[1], dtype=jnp.float32)
    for l in range(DEPTH):
        m = mixing_sublayer(x, pos, w_in[l], b_in[l], conv_w[l], conv_b[l], conv_ln_g[l], conv_ln_b[l],
                            attn_sinks[l], gmlp_ln_g[l], gmlp_ln_b[l], gmlp_w_s[l], gmlp_b_s[l],
                            w_out[l], b_out[l])
        x = layer_norm(DN_ALPHA * x + m, ln_mix_g[l], ln_mix_b[l])
        f = moe_ffn(x, w_router, router_bias, exp_w_gate[l], exp_w_up[l], exp_w_down[l])
        x = layer_norm(DN_ALPHA * x + f, ln_ffn_g[l], ln_ffn_b[l])
    return x


_drawn_inputs = setup_inputs


def setup_inputs(seed=0):
    import zlib

    import numpy as np

    out = dict(_drawn_inputs(seed))
    spreads = {}
    factors = {'conv_b': 3.059,
     'conv_ln_g': 4.06,
     'conv_ln_b': 5.261,
     'attn_sinks': 29.626,
     'gmlp_ln_g': 5.831,
     'gmlp_ln_b': 7.469,
     'gmlp_b_s': 5.387}
    for name, (base, spread) in spreads.items():
        noise = np.random.default_rng([zlib.crc32(name.encode()), seed]).standard_normal(out[name].shape)
        drawn = base * np.exp(spread * noise) if base else spread * noise
        out[name] = __import__('jax').numpy.asarray(drawn.astype(out[name].dtype))
    for name, factor in factors.items():
        out[name] = (out[name] * factor).astype(out[name].dtype)
    return out
```

```python
from contextlib import ExitStack

import numpy as np

import concourse.bass as bass
from concourse import mybir

F32 = mybir.dt.float32
BF16 = mybir.dt.bfloat16
I32 = mybir.dt.int32
ALU = mybir.AluOpType
ACT = mybir.ActivationFunctionType
AX = mybir.AxisListType

P = 128
D = 1024
KD = D // P
T = 512
TT = T // P
DEPTH = 2
CONV = 256
TAPS = 31
HD = 64
NQ = 8
NKV = 2
ROPE = HD // 4
THETA = 500000.0
GM = 256
GH = 4
D_IN = 2 * CONV + NQ * HD + 2 * NKV * HD + 2 * GM
E = 16
G = 4
EG = E // G
FE = D // 2
KF = FE // P
EPS = 1e-5
ALPHA = (2 * DEPTH) ** 0.25
PIECE = 256
NPIECE = D_IN // PIECE
MAXCH = 48
OOB = 4096
C_BIN, C_CW, C_CB, C_CG, C_CLB, C_SINK, C_RB = 0, 14, 76, 78, 80, 82, 90
NCOL = 106
K_ID, K_PERM, K_UTRI, K_IOTA, K_KE, K_KG, K_DEST, K_COS, K_SIN = 0, 128, 256, 384, 512, 528, 532, 540, 540 + T
NCONST = 540 + 2 * T
PROJ = 15
PROJ_ACT = (0, 2, 4, 5, 6, 7, 8, 13, 14)
PROJ_DVE = (1, 3, 9, 10, 11, 12)


def build(nc, a):
    ctx = ExitStack()
    with ctx:
        def sem(name):
            return ctx.enter_context(nc.semaphore(name))

        wexp = [[ctx.enter_context(nc.sbuf_tensor(f"w_{n}{r}", [P, 4096], F32)) for n in ("gate", "up", "down")]
                for r in range(2)]
        wg = [wexp[r][0][:, :].rearrange("p (k n) -> p k n", k=KD) for r in range(2)]
        wu = [wexp[r][1][:, :].rearrange("p (k n) -> p k n", k=KD) for r in range(2)]
        wd = [wexp[r][2][:, :].rearrange("p (k n) -> p k n", k=KF) for r in range(2)]
        xT = ctx.enter_context(nc.sbuf_tensor("xT", [P, KD, T], F32))
        xtok = ctx.enter_context(nc.sbuf_tensor("xtok", [P, TT, D], F32))
        catmem = ctx.enter_context(nc.sbuf_tensor("catmem", [P, KD * T], F32))
        winmem = ctx.enter_context(nc.sbuf_tensor("winmem", [P, 4096], F32))
        cat = catmem[:, :].rearrange("p (k t) -> p k t", k=KD)
        win = [winmem[:, 2048 * r:2048 * r + 2048].rearrange("p (k n) -> p k n", k=KD) for r in range(2)]
        wout = [winmem[:, :].rearrange("p (k n) -> p k n", k=KD), wexp[1][2][:, :].rearrange("p (k n) -> p k n", k=KD)]

        gluP = ctx.enter_context(nc.sbuf_tensor("gluP", [P, 2 * (T + TAPS - 1)], F32))
        glu = gluP[:, :].rearrange("p (m t) -> p m t", m=2)
        Pm = gluP[:, 0:1024].rearrange("p (h k) -> p h k", h=NQ)
        tmp = ctx.enter_context(nc.sbuf_tensor("tmp", [P, 1024], F32))
        qkg = ctx.enter_context(nc.sbuf_tensor("qkg", [P, 3584], F32))
        qr = qkg[:, 0:2048].rearrange("p (m t) -> p m t", m=4)
        gv = qkg[:, 2048:3072].rearrange("p (j c) -> p j c", j=TT)
        kr = qkg[:, 3072:3584]
        rows3 = qkg[:, 0:3072].rearrange("p (r n) -> p r n", r=3)
        vmem = ctx.enter_context(nc.sbuf_tensor("vmem", [P, 2, TT, P], F32))
        u = ctx.enter_context(nc.sbuf_tensor("u", [P, 2, T], F32))
        wsT = ctx.enter_context(nc.sbuf_tensor("wsT", [P, GH, P], F32))
        bsp = ctx.enter_context(nc.sbuf_tensor("bsp", [P, 2, P], F32))
        cst = ctx.enter_context(nc.sbuf_tensor("cst", [P, NCONST], F32))
        col = ctx.enter_context(nc.sbuf_tensor("col", [P, NCOL], F32))
        rowm = ctx.enter_context(nc.sbuf_tensor("rowm", [P, 896], F32))
        wr = ctx.enter_context(nc.sbuf_tensor("wr", [P, KD, E], F32))
        ident = cst[:, K_ID:K_ID + P]
        perm = cst[:, K_PERM:K_PERM + P]
        PT = cst[:, K_COS:K_COS + 2 * T].rearrange("p (h q) -> p h q", h=NQ)
        cosT = cst[:, K_COS:K_COS + T]
        sinT = cst[:, K_SIN:K_SIN + T]
        onesc = ctx.enter_context(nc.sbuf_tensor("onesc", [P, P], F32))
        onesb = ctx.enter_context(nc.sbuf_tensor("onesb", [P, P], BF16))
        utri = ctx.enter_context(nc.sbuf_tensor("utri", [P, P], BF16))
        selb = ctx.enter_context(nc.sbuf_tensor("selb", [P, TT, E], BF16))
        small = ctx.enter_context(nc.sbuf_tensor("small", [P, 160], F32))
        startf = ctx.enter_context(nc.sbuf_tensor("startf", [P, DEPTH, E + 1], F32))
        starti = ctx.enter_context(nc.sbuf_tensor("starti", [P, DEPTH * (E + 1)], I32))
        toki = ctx.enter_context(nc.sbuf_tensor("toki", [P, MAXCH], I32))
        dsti = ctx.enter_context(nc.sbuf_tensor("dsti", [P, MAXCH], I32))
        gatef = ctx.enter_context(nc.sbuf_tensor("gatef", [P, MAXCH], F32))
        gather_idx = ctx.enter_context(nc.sbuf_tensor("gather_idx", [P, 1], I32))
        scatter_idx = ctx.enter_context(nc.sbuf_tensor("scatter_idx", [P, 1], I32))
        gate_cur = ctx.enter_context(nc.sbuf_tensor("gate_cur", [P, 1], F32))
        eps = small[:, 0:1]
        mhalf = small[:, 1:5]
        bn6 = small[:, 8:32]
        mv = small[:, 32:40]
        ve = small[:, 40:44]
        rstd = small[:, 44:48]
        smax, snmax, ses, ssum = ([small[:, 48 + 32 * b + 8 * i:56 + 32 * b + 8 * i] for b in range(2)]
                                  for i in range(4))
        xg = winmem[:, 0:1024]
        xgT = winmem[:, 1024:2048].rearrange("p (k t) -> p k t", k=KD)
        ysb = winmem[:, 2048:3072]
        sg = winmem[:, 3072:3584]
        he = winmem[:, 3584:4096]
        heT = tmp[:, 0:512].rearrange("p (k t) -> p k t", k=KF)
        lg, ex, sel, smk, key, oh1, oh2, kk = (
            catmem[:, 64 * i:64 * i + 64].rearrange("p (j e) -> p j e", j=TT) for i in range(8))
        pr = catmem[:, 512:608].rearrange("p (g m) -> p g m", m=6)
        gsc, gkey, ing = (catmem[:, 608 + 16 * i:624 + 16 * i].rearrange("p (j g) -> p j g", j=TT) for i in range(3))
        r4 = [catmem[:, 656 + 4 * i:660 + 4 * i] for i in range(6)]
        nch = catmem[:, 680:696]
        zero16 = catmem[:, 696:712]
        rk = catmem[:, 712:720]
        stc = catmem[:, 720:728]
        ovf = catmem[:, 728:736]
        gt = catmem[:, 736:744]
        tabf = catmem[:, 752:752 + MAXCH]
        tab2 = catmem[:, 800:800 + MAXCH]
        hotA = catmem[:, 1024:2048].rearrange("p (q s) -> p q s", q=8)
        hotB = catmem[:, 2048:2048 + 8 * 2 * MAXCH].rearrange("p (q v c) -> p q v c", q=8, v=2)
        ycomb = [catmem[:, 2048 * i:2048 * i + 2048].rearrange("p (r n) -> p r n", r=2) for i in range(2)]

        bank = [ctx.enter_context(nc.psum_tensor(f"bank{i}", [P, 512], F32)) for i in range(8)]

        x1d = [nc.dram_tensor(f"x1_rows{l}", [T, D], F32, kind="Internal").ap() for l in range(DEPTH)]
        yd = [nc.dram_tensor(f"y_rows{l}", [2 * T, D], F32, kind="Internal").ap() for l in range(DEPTH)]

        const_in, ones_set, angles_in = sem("const_in"), sem("ones_set"), sem("angles_in")
        col_in, row_in, gm_in = sem("col_in"), sem("row_in"), sem("gm_in")
        xT_in, xtok_in = sem("xT_in"), sem("xtok_in")
        win_in = [sem(f"win_in{i}") for i in range(2)]
        wout_in = [sem(f"wout_in{i}") for i in range(2)]
        rows_in = sem("rows_in")
        wexp_in = [[sem(f"{n}_in{r}") for n in ("gate", "up", "down")] for r in range(2)]
        act_chain, dve_chain, pool_chain = sem("act_chain"), sem("dve_chain"), sem("pool_chain")
        proj_done = sem("proj_done")
        proj_act, proj_dve = sem("proj_act"), sem("proj_dve")
        sig_set, glu_read, rot_done, rot_used = sem("sig_set"), sem("glu_read"), sem("rot_done"), sem("rot_used")
        conv_acc, mean_done, cen_set, sq_set, var_done, sd_set, conv_norm, conv_cat = (
            sem(n) for n in ("conv_acc", "mean_done", "cen_set", "sq_set", "var_done", "sd_set", "conv_norm",
                             "conv_cat"))
        v_set, voff_in = sem("v_set"), sem("voff_in")
        gvb_set, gv_act, gvar_set, grstd_set, gvh_set, gvn_set, gm_done, gm_cat = (
            sem(n) for n in ("gvb_set", "gv_act", "gvar_set", "grstd_set", "gvh_set", "gvn_set", "gm_done",
                             "gm_cat"))
        mask_set, s_done, s_max, p_done, pn_done, pt_done, pt_act, pt_dve, o_done, o_used = (
            sem(n) for n in ("mask_set", "s_done", "s_max", "p_done", "pn_done", "pt_done", "pt_act", "pt_dve",
                             "o_done", "o_used"))
        xb_done, op_done, op_used = sem("xb_done"), sem("op_done"), sem("op_used")
        ln_var, ln_rstd, ln_norm, ln_out = sem("ln_var"), sem("ln_rstd"), sem("ln_norm"), sem("ln_out")
        x1_stored, tr_done, tr_used = sem("x1_stored"), sem("tr_done"), sem("tr_used")
        lg_done, rt_sub, rt_exp, rt_sel, rk_done, rt_hot, tab_done, tab_set = (
            sem(n) for n in ("lg_done", "rt_sub", "rt_exp", "rt_sel", "rk_done", "rt_hot", "tab_done", "tab_set"))
        idx_set, gathered = sem("idx_set"), sem("gathered")
        dst_set = sem("dst_set")
        gather_sent, scatter_sent = sem("gather_sent"), sem("scatter_sent")
        cur_set, scattered = sem("cur_set"), sem("scattered")
        xg_turned, xgT_act, xgT_dve = sem("xg_turned"), sem("xgT_act"), sem("xgT_dve")
        gate_used, up_used, down_used = sem("gate_used"), sem("up_used"), sem("down_used")
        sg_set, he_set, he_turned, heT_set, y_act, y_dve = (
            sem(n) for n in ("sg_set", "he_set", "he_turned", "heT_set", "y_act", "y_dve"))
        y_in = [sem(f"y_in{i}") for i in range(2)]
        y_added, out_stored = sem("y_added"), sem("out_stored")

        block = ctx.enter_context(nc.Block())

        def first_chunk(eng, l, e):
            return eng.value_load(starti[0:1, bass.ds(l * (E + 1) + e, 1)], min_val=0, max_val=MAXCH - 1)

        @block.sync
        def _(sp):
            def gmlp_params(l):
                ws = a["ws_t"][l].rearrange("h j i -> j h i")
                sp.dma_start(wsT[0:64, :, :], ws[0:64, :, :]).then_inc(gm_in, 16)
                sp.dma_start(wsT[64:P, :, 64:P], ws[64:P, :, 64:P]).then_inc(gm_in, 16)
                for m in range(2):
                    for g in range(2):
                        sp.dma_start(bsp[64 * g:64 * g + 64, m, :],
                                     a["gmlp_b_s"][l, 2 * m + g].partition_broadcast(64)).then_inc(gm_in, 16)

            def small_params(l):
                sp.dma_start(col[:, :], a["cols"][l]).then_inc(col_in, 16)
                sp.dma_start(rowm[:, :], a["rowm"][l].partition_broadcast(P)).then_inc(row_in, 16)
                gmlp_params(l)

            def load_win(l, i):
                sp.dma_start(win[i % 2], a["w_in"][l, :, i * PIECE:(i + 1) * PIECE]
                             .rearrange("(k p) n -> p k n", p=P)).then_inc(win_in[i % 2], 16)

            def load_wout(l, n):
                sp.dma_start(wout[n], a["w_out"][l, :, 512 * n:512 * n + 512]
                             .rearrange("(k p) n -> p k n", p=P)).then_inc(wout_in[n], 16)

            def load_expert(l, e, r, piece):
                w = a[("exp_w_gate", "exp_w_up", "exp_w_down")[piece]]
                sp.dma_start((wg, wu, wd)[piece][r], w[bass.ds(l * E + e, 1), :, :]
                             .rearrange("o (k p) n -> p (o k) n", p=P)).then_inc(wexp_in[r][piece], 16)

            for l in range(DEPTH):
                if l == 0:
                    sp.dma_start(col[:, :], a["cols"][l]).then_inc(col_in, 16)
                    load_win(l, 0)
                    sp.dma_start(xT[:, :, :], a["x_t"].rearrange("(k p) t -> p k t", p=P)).then_inc(xT_in, 16)
                    load_win(l, 1)
                    sp.dma_start(cst[:, :], a["const"]).then_inc(const_in, 16)
                    sp.dma_start(wr[:, :, :], a["w_router"].rearrange("(k p) e -> p k e", p=P)).then_inc(const_in, 16)
                    sp.dma_start(xtok[:, :, :], a["x"].rearrange("(j p) n -> p j n", p=P)).then_inc(xtok_in, 16)
                    sp.dma_start(rowm[:, :], a["rowm"][l].partition_broadcast(P)).then_inc(row_in, 16)
                    gmlp_params(l)
                else:
                    for r in range(2):
                        done = first_chunk(sp, l - 1, E - 1 + r)
                        for piece, used in enumerate((gate_used, up_used, down_used)):
                            if (r, piece) != (1, 2):
                                sp.wait_ge(used, done)
                                load_expert(l, r, r, piece)
                    small_params(l)
                    sp.wait_ge(o_done, TT * l)
                    sp.dma_start(cst[:, K_COS:], a["const"][:, K_COS:]).then_inc(angles_in, 16)
                    done = first_chunk(sp, l - 1, E)
                    sp.wait_ge(scattered, done * 16)
                    load_win(l, 0)
                    load_win(l, 1)
                for i in range(2, NPIECE):
                    sp.wait_ge(proj_done, l * PROJ + (3, 4, 6, 8, 13)[i - 2])
                    load_win(l, i)
                    if i == 3:
                        load_wout(l, 1)
                    if l == 0 and i in (4, 5):
                        for piece in range(3 if i == 4 else 2):
                            load_expert(l, i - 4, i - 4, piece)
                sp.wait_ge(proj_done, l * PROJ + PROJ)
                load_wout(l, 0)
                sp.wait_ge(s_done, TT * (l + 1))
                sp.wait_ge(gm_done, 2 * (l + 1))
                sp.dma_start(rows3, a["rows_mix"][l].partition_broadcast(P)).then_inc(rows_in, 16)
                sp.wait_ge(op_done, TT * (l + 1))
                load_expert(l, 1, 1, 2)
                sp.wait_ge(ln_out, TT * (2 * l + 1))
                sp.dma_start(rows3[:, 0:2, :], a["rows_ffn"][l].partition_broadcast(P)).then_inc(rows_in, 16)
                sp.wait_ge(tab_set, l + 1)
                with sp.Fori(1, E // 2) as pair:
                    for r in range(2):
                        e = 2 * pair + r
                        done = first_chunk(sp, l, e - 1)
                        for piece, used in enumerate((gate_used, up_used, down_used)):
                            sp.wait_ge(used, done)
                            load_expert(l, e, r, piece)

        @block.tensor
        def _(pe):
            def project(l):
                task = [0]

                def free(t):
                    if t >= 4 and t - 4 in PROJ_ACT:
                        pe.wait_ge(proj_act, l * len(PROJ_ACT) + PROJ_ACT.index(t - 4) + 1)
                    elif t >= 4:
                        pe.wait_ge(proj_dve, l * len(PROJ_DVE) + PROJ_DVE.index(t - 4) + 1)

                def piece(i):
                    n = (NPIECE + 1) // 2 if i % 2 == 0 else NPIECE // 2
                    pe.wait_ge(win_in[i % 2], 16 * (l * n + i // 2 + 1))

                def channels(i, m):
                    t = task[0]
                    free(t)
                    for k in range(KD):
                        mm = pe.matmul(bank[t % 4][:, :], win[i % 2][:, k, P * m:P * m + P], xT[:, k, :],
                                       start=(k == 0), stop=(k == KD - 1))
                    mm.then_inc(proj_done, 1)
                    task[0] += 1

                def rotate(n, src):
                    pe.wait_ge(proj_act, l * len(PROJ_ACT) + 3 + n)
                    if n == 4:
                        pe.wait_ge(rot_used, 5 * l + 1)
                    pe.matmul(bank[4 + n % 4][:, :], perm, src, start=True, stop=True).then_inc(rot_done, 1)

                def tokens(j):
                    t = task[0]
                    free(t)
                    for r, c, n, o in ((0, P, P, 0), (1, 0, GM, P)):
                        for k in range(KD):
                            mm = pe.matmul(bank[t % 4][:, o:o + n], xT[:, k, P * j:P * j + P],
                                           win[r][:, k, c:c + n], start=(k == 0), stop=(k == KD - 1))
                    mm.then_inc(proj_done, 1)
                    task[0] += 1

                if l == 0:
                    pe.wait_ge(xT_in, 16)
                else:
                    pe.wait_ge(tr_used, 2 * TT * 2 * l)
                piece(0)
                channels(0, 0)
                piece(1)
                channels(1, 0)
                channels(0, 1)
                channels(1, 1)
                if l == 0:
                    pe.wait_ge(const_in, 32)
                    pe.wait_ge(ones_set, 4)
                piece(2)
                channels(2, 0)
                channels(2, 1)
                rotate(0, qr[:, 0, :])
                piece(3)
                channels(3, 0)
                rotate(1, qr[:, 1, :])
                channels(3, 1)
                rotate(2, qr[:, 2, :])
                piece(4)
                channels(4, 0)
                rotate(3, qr[:, 3, :])
                piece(5)
                tokens(0)
                rotate(4, kr)
                tokens(1)
                pe.wait_ge(conv_acc, 2 * (l + 1))
                pe.wait_ge(rot_used, 5 * l + 2)
                for m in range(2):
                    mm = pe.matmul(bank[5][:, :], onesc[:, :], cat[:, m, :], start=(m == 0), stop=(m == 1))
                mm.then_inc(mean_done, 1)
                tokens(2)
                tokens(3)
                piece(6)
                channels(6, 0)
                pe.wait_ge(sq_set, 2 * (l + 1))
                pe.wait_ge(rot_used, 5 * l + 3)
                for m in range(2):
                    mm = pe.matmul(bank[6][:, :], onesc[:, :], tmp[:, T * m:T * m + T], start=(m == 0), stop=(m == 1))
                mm.then_inc(var_done, 1)
                channels(6, 1)

            def scores(l, b):
                n = TT * l + b
                if b == 0:
                    pe.wait_ge(rot_used, 5 * (l + 1))
                    pe.wait_ge(mask_set, l + 1)
                elif b == 1:
                    pe.wait_ge(sd_set, l + 1)
                else:
                    pe.wait_ge(p_done, n - 1)
                for c in (2 * b, 2 * b + 1):
                    for g in range(2):
                        for m in range(4):
                            o, h = (64, 64) if c == 0 else (0, P)
                            mm = pe.matmul(bank[4 + 2 * (b % 2) + g][64 * (c % 2):64 * (c % 2) + 64, P * m + o:P * m + P],
                                           qr[64 * g:64 * g + 64, m, 64 * c:64 * c + 64],
                                           kr[64 * g:64 * g + 64, 64 * c + 64 - h:64 * c + 64], start=True, stop=True)
                mm.then_inc(s_done, 1)

            def attend(l, b):
                n = TT * l + b
                pe.wait_ge(pn_done, n + 1)
                if b > 0:
                    pe.wait_ge(pt_act, n)
                    pe.wait_ge(pt_dve, n)
                else:
                    pe.wait_ge(proj_act, len(PROJ_ACT) * (l + 1))
                    pe.wait_ge(proj_dve, len(PROJ_DVE) * (l + 1))
                for h in range(NQ):
                    mm = pe.transpose(bank[h // 4][:, P * (h % 4):P * (h % 4) + P], Pm[:, h, :], ident)
                mm.then_inc(pt_done, 1)
                pe.wait_ge(pt_act, n + 1)
                pe.wait_ge(pt_dve, n + 1)
                if b > 0:
                    pe.wait_ge(o_used, n)
                else:
                    pe.wait_ge(voff_in, 64 * (l + 1))
                for c in range(2):
                    for g in range(2):
                        mm = pe.matmul(bank[2][64 * g:64 * g + 64, 256 * c:256 * c + 256],
                                       vmem[:, 1 - c, b, 64 * g:64 * g + 64],
                                       PT[:, 4 * g:4 * g + 4, 64 * c:64 * c + 64], start=True, stop=True)
                mm.then_inc(o_done, 1)

            def spatial(l, m):
                pe.wait_ge(gvn_set, l + 1)
                pe.wait_ge(gm_in, 96 * (l + 1))
                pe.wait_ge(ones_set, 4)
                if m == 1:
                    pe.wait_ge(gm_cat, 2 * l + 1)
                for j in range(TT):
                    for g in range(2):
                        h = 2 * m + g
                        mm = pe.matmul(bank[3][64 * g:64 * g + 64, P * j:P * j + P], gv[:, j, 64 * h:64 * h + 64],
                                       wsT[:, h, :], start=True, stop=True)
                mm.then_inc(gm_done, 1)

            def project_out(l):
                pe.wait_ge(o_used, TT * (l + 1))
                pe.wait_ge(gm_cat, 2 * (l + 1))
                pe.wait_ge(conv_cat, 2 * (l + 1))
                for n in range(2):
                    pe.wait_ge(wout_in[n], 16 * (l + 1))
                for j in range(TT):
                    if j >= 2:
                        pe.wait_ge(op_used, TT * l + j - 1)
                    for n in range(2):
                        for k in range(KD):
                            mm = pe.matmul(bank[2 * (j % 2) + n][:, :], cat[:, k, P * j:P * j + P], wout[n][:, k, :],
                                           start=(k == 0), stop=(k == KD - 1))
                    mm.then_inc(op_done, 1)
                    if j >= 1:
                        turn(2 * l, j - 1)
                turn(2 * l, TT - 1)

            def turn(q, j):
                pe.wait_ge(ln_out, TT * q + j + 1)
                if j >= 2:
                    pe.wait_ge(tr_used, 2 * (TT * q + j - 1))
                for k in range(KD):
                    mm = pe.transpose(bank[4 + 2 * (j % 2) + k // 4][:, P * (k % 4):P * (k % 4) + P],
                                      xtok[:, j, P * k:P * k + P], ident)
                mm.then_inc(tr_done, 1)

            def route(l):
                pe.wait_ge(tr_used, 2 * TT * (2 * l + 1))
                pe.wait_ge(op_used, TT * (l + 1))
                for j in range(TT):
                    for k in range(KD):
                        mm = pe.matmul(bank[0][:, E * j:E * j + E], xT[:, k, P * j:P * j + P], wr[:, k, :],
                                       start=(k == 0), stop=(k == KD - 1))
                mm.then_inc(lg_done, 1)
                pe.wait_ge(rt_sel, l + 1)
                for j in range(TT + 1):
                    own = j < TT
                    for i in range(j):
                        mm = pe.matmul(bank[1][:, E * j:E * j + E], onesb[:, :], selb[:, i, :],
                                       start=(i == 0), stop=(not own and i == j - 1))
                    if own:
                        pe.matmul(bank[1][:, E * j:E * j + E], utri[:, :], selb[:, j, :], start=(j == 0), stop=True)
                mm.then_inc(rk_done, 1)
                pe.wait_ge(rt_hot, l + 1)
                for q in range(2 * TT):
                    mm = pe.matmul(bank[2][:, 0:2 * MAXCH], hotA[:, q, :], hotB[:, q, :, :],
                                   start=(q == 0), stop=(q == 2 * TT - 1))
                mm.then_inc(tab_done, 1)

            def turn_gathered(c, l):
                pe.wait_ge(gathered, (c + (l + 1)) * 16)
                for k in range(KD):
                    mm = pe.transpose(bank[2 + k // 4][:, P * (k % 4):P * (k % 4) + P], xg[:, P * k:P * k + P], ident)
                mm.then_inc(xg_turned, 1)

            def chunk(l, c, pair, r):
                landed = (pair + (l * (E // 2) + 1)) * 16
                pe.wait_ge(xgT_act, c + (l + 1))
                pe.wait_ge(xgT_dve, c + (l + 1))
                pe.wait_ge(he_set, c)
                pe.wait_ge(wexp_in[r][0], landed)
                for k in range(KD):
                    mm = pe.matmul(bank[0][:, :], xgT[:, k, :], wg[r][:, k, :], start=(k == 0), stop=(k == KD - 1))
                mm.then_inc(gate_used, 1)
                pe.wait_ge(wexp_in[r][1], landed)
                for k in range(KD):
                    mm = pe.matmul(bank[1][:, :], xgT[:, k, :], wu[r][:, k, :], start=(k == 0), stop=(k == KD - 1))
                mm.then_inc(up_used, 1)
                turn_gathered(c + 1, l)
                pe.wait_ge(he_set, c + 1)
                for k in range(KF):
                    mm = pe.transpose(bank[4][:, P * k:P * k + P], he[:, P * k:P * k + P], ident)
                mm.then_inc(he_turned, 1)
                pe.wait_ge(wexp_in[r][2], landed)
                pe.wait_ge(heT_set, c + 1)
                pe.wait_ge(y_act, c)
                pe.wait_ge(y_dve, c)
                for n in range(2):
                    for k in range(KF):
                        mm = pe.matmul(bank[5 + n][:, :], heT[:, k, :], wd[r][:, k, 512 * n:512 * n + 512],
                                       start=(k == 0), stop=(k == KF - 1))
                mm.then_inc(down_used, 1)

            for l in range(DEPTH):
                project(l)
                scores(l, 0)
                scores(l, 1)
                attend(l, 0)
                scores(l, 2)
                attend(l, 1)
                spatial(l, 0)
                spatial(l, 1)
                scores(l, 3)
                attend(l, 2)
                attend(l, 3)
                project_out(l)
                route(l)
                pe.wait_ge(tab_set, l + 1)
                turn_gathered(first_chunk(pe, l, 0), l)
                with pe.Fori(0, E // 2) as pair:
                    for r in range(2):
                        lo = first_chunk(pe, l, 2 * pair + r)
                        hi = first_chunk(pe, l, 2 * pair + (r + 1))
                        with pe.Fori(lo, hi) as c:
                            chunk(l, c, pair, r)
                if l + 1 < DEPTH:
                    for j in range(TT):
                        turn(2 * l + 1, j)

        @block.scalar
        def _(act):
            def bias(i):
                return col[:, C_BIN + i:C_BIN + i + 1]

            def project(l):
                def tile(t):
                    act.wait_ge(proj_done, PROJ * l + t + 1)
                    return bank[t % 4][:, :]

                act.wait_ge(col_in, 16 * (l + 1))
                for m in range(2):
                    src = tile(2 * m)
                    act.activation(u[:, m, :], src, ACT.Sigmoid, bias=bias(m)).then_inc(sig_set, 1)
                    act.wait_ge(sig_set, 2 * l + m + 1)
                    act.sem_inc(proj_act, 1)
                for m in range(4):
                    src = tile(4 + m)
                    act.activation(qr[:, m, :], src, ACT.Identity, bias=bias(4 + m)).then_inc(proj_act, 1)
                src = tile(8)
                act.activation(kr, src, ACT.Identity, bias=bias(8)).then_inc(proj_act, 1)
                for j in range(TT):
                    act.wait_ge(gvb_set, TT * l + j + 1)
                    act.activation(gv[:, j, :], gv[:, j, :], ACT.Gelu_apprx_tanh).then_inc(gv_act, 1)
                act.wait_ge(glu_read, 2 * (l + 1))
                src = tile(13)
                act.activation(u[:, 0, :], src, ACT.Gelu_apprx_tanh, bias=bias(12)).then_inc(proj_act, 1)
                for m in range(2):
                    act.wait_ge(cen_set, 2 * l + m + 1)
                    act.activation(tmp[:, T * m:T * m + T], cat[:, m, :], ACT.Square).then_inc(sq_set, 1)
                src = tile(14)
                act.activation(u[:, 1, :], src, ACT.Gelu_apprx_tanh, bias=bias(13)).then_inc(proj_act, 1)
                act.wait_ge(var_done, l + 1)
                act.activation(tmp[:, 0:T], bank[6][:, :], ACT.Sqrt, bias=eps).then_inc(sd_set, 1)

            def softmax(l, b):
                n = TT * l + b
                act.wait_ge(s_max, n + 1)
                if b > 0:
                    act.wait_ge(pt_done, n)
                else:
                    act.wait_ge(conv_acc, 2 * (l + 1))
                act.activation(ses[b % 2], ses[b % 2], ACT.Exp)
                for h in range(NQ):
                    x = act.activation(Pm[:, h, :], bank[4 + 2 * (b % 2) + h // 4][:, P * (h % 4):P * (h % 4) + P],
                                       ACT.Exp, bias=snmax[b % 2][:, h:h + 1], scale=HD ** -0.5,
                                       accum_out=ssum[b % 2][:, h:h + 1])
                x.then_inc(p_done, 1)

            def copy_turned(l, b):
                n = TT * l + b
                act.wait_ge(pt_done, n + 1)
                if b > 0:
                    act.wait_ge(o_done, n)
                act.activation(PT[:, 0:4, :], bank[0][:, :].rearrange("p (h q) -> p h q", h=4), ACT.Copy)\
                   .then_inc(pt_act, 1)

            def copy_heads(l, b):
                n = TT * l + b
                act.wait_ge(o_done, n + 1)
                act.activation(cat[:, 2:6, P * b:P * b + P].rearrange("p m (c q) -> p m c q", c=2),
                               bank[2][:, :].rearrange("p (c m q) -> p m c q", c=2, m=4), ACT.Copy).then_inc(o_used, 1)

            def copy_xT(q, j):
                act.wait_ge(tr_done, TT * q + j + 1)
                for i in range(2):
                    act.activation(xT[:, 4 * i:4 * i + 4, P * j:P * j + P],
                                   bank[4 + 2 * (j % 2) + i][:, :].rearrange("p (k t) -> p k t", k=4), ACT.Copy)\
                       .then_inc(tr_used, 1)

            def copy_gathered(c, l):
                act.wait_ge(xg_turned, c + (l + 1))
                act.activation(xgT[:, 0:4, :], bank[2][:, :].rearrange("p (k t) -> p k t", k=4), ACT.Copy)\
                   .then_inc(xgT_act, 1)

            for l in range(DEPTH):
                project(l)
                softmax(l, 0)
                for b in range(TT):
                    copy_turned(l, b)
                    if b + 1 < TT:
                        softmax(l, b + 1)
                    copy_heads(l, b)
                for m in range(2):
                    act.wait_ge(conv_norm, 2 * l + m + 1)
                    act.activation(cat[:, m, :], cat[:, m, :], ACT.Silu, bias=col[:, C_CLB + m:C_CLB + m + 1],
                                   scale=col[:, C_CG + m:C_CG + m + 1]).then_inc(conv_cat, 1)
                for j in range(TT):
                    copy_xT(2 * l, j)
                act.wait_ge(rt_sub, l + 1)
                act.activation(ex, lg, ACT.Exp).then_inc(rt_exp, 1)
                act.wait_ge(tab_set, l + 1)
                copy_gathered(first_chunk(act, l, 0), l)
                with act.Fori(first_chunk(act, l, 0), first_chunk(act, l, E)) as c:
                    act.wait_ge(gate_used, c + 1)
                    act.wait_ge(he_set, c)
                    act.activation(sg, bank[0][:, :], ACT.Silu).then_inc(sg_set, 1)
                    act.wait_ge(he_turned, c + 1)
                    act.wait_ge(down_used, c)
                    act.activation(heT, bank[4][:, :].rearrange("p (k t) -> p k t", k=KF), ACT.Copy)\
                       .then_inc(heT_set, 1)
                    act.wait_ge(up_used, c + 1)
                    copy_gathered(c + 1, l)
                    act.wait_ge(down_used, c + 1)
                    act.wait_ge(cur_set, c + 1)
                    act.wait_ge(scattered, c * 16)
                    act.activation(ysb[:, 0:512], bank[5][:, :], ACT.Copy, scale=gate_cur[:, :]).then_inc(y_act, 1)
                act.wait_ge(scattered, first_chunk(act, l, E) * 16)
                for j in range(TT):
                    if j >= 2:
                        act.wait_ge(y_added, TT * l + j - 1)
                    act.dma_start(ycomb[j % 2], yd[l].rearrange("(r j p) n -> j p r n", r=2, p=P)[j])\
                       .then_inc(y_in[j % 2], 16)
                if l + 1 < DEPTH:
                    for j in range(TT):
                        copy_xT(2 * l + 1, j)

        @block.vector
        def _(dve):
            chain = [0]

            def link(x):
                chain[0] += 1
                x.then_inc(dve_chain, 1)
                dve.wait_ge(dve_chain, chain[0])

            def norm_stats(src, j, halves):
                for i, s in enumerate(src):
                    link(dve.bn_stats(bn6[:, 6 * i:6 * i + 6], s))
                link(dve.bn_aggr(mv[:, 2 * j:2 * j + 2], bn6[:, 0:6 * halves]))

            def rope(l, n, x):
                dve.wait_ge(rot_done, 5 * l + n + 1)
                if l > 0:
                    dve.wait_ge(angles_in, 16 * l)
                link(dve.tensor_tensor(tmp[:, 0:T], bank[4 + n % 4][:, :], sinT, ALU.mult))
                link(dve.tensor_tensor(x, x, cosT, ALU.mult))
                link(dve.tensor_tensor(x, x, tmp[:, 0:T], ALU.add))
                dve.sem_inc(rot_used, 1)

            def conv(l):
                link(dve.memset(glu[:, :, 0:TAPS - 1], 0.0))
                for m in range(2):
                    dve.wait_ge(proj_done, PROJ * l + 2 * m + 2)
                    dve.wait_ge(sig_set, 2 * l + m + 1)
                    link(dve.scalar_tensor_tensor(glu[:, m, TAPS - 1:], bank[2 * m + 1][:, :],
                                                  col[:, C_BIN + 2 + m:C_BIN + 3 + m], u[:, m, :], ALU.add, ALU.mult))
                    dve.sem_inc(proj_dve, 1)
                    dve.sem_inc(glu_read, 1)
                    w = C_CW + TAPS * m
                    link(dve.tensor_scalar(cat[:, m, :], glu[:, m, 0:T], col[:, w:w + 1],
                                           col[:, C_CB + m:C_CB + m + 1], ALU.mult, ALU.add))
                    for k in range(1, TAPS):
                        link(dve.scalar_tensor_tensor(cat[:, m, :], glu[:, m, k:k + T], col[:, w + k:w + k + 1],
                                                      cat[:, m, :], ALU.mult, ALU.add))
                    dve.sem_inc(conv_acc, 1)

            def tokens(l, j):
                t = 9 + j
                dve.wait_ge(proj_done, PROJ * l + t + 1)
                dve.wait_ge(row_in, 16 * (l + 1))
                dve.tensor_tensor(vmem[:, 0, j, :], bank[t % 4][:, 0:P], rowm[:, 0:P], ALU.add).then_inc(v_set, 1)
                dve.tensor_tensor(gv[:, j, :], bank[t % 4][:, P:P + GM], rowm[:, P:P + GM], ALU.add).then_inc(gvb_set, 1)
                dve.wait_ge(gvb_set, TT * l + j + 1)
                dve.wait_ge(v_set, TT * l + j + 1)
                dve.sem_inc(proj_dve, 1)

            def softmax_max(l, b):
                n = TT * l + b
                i = b % 2
                dve.wait_ge(s_done, n + 1)
                for g in range(2):
                    link(dve.tensor_reduce(smax[i][:, 4 * g:4 * g + 4],
                                           bank[4 + 2 * i + g][:, :].rearrange("p (h k) -> p h k", h=4), AX.X, ALU.max))
                link(dve.scalar_tensor_tensor(smax[i], smax[i], HD ** -0.5, col[:, C_SINK:C_SINK + NQ],
                                              ALU.mult, ALU.max))
                dve.tensor_scalar(snmax[i], smax[i], -1.0, None, ALU.mult)
                link(dve.tensor_tensor(ses[i], col[:, C_SINK:C_SINK + NQ], smax[i], ALU.subtract))
                dve.sem_inc(s_max, 1)

            def softmax_norm(l, b):
                n = TT * l + b
                i = b % 2
                dve.wait_ge(p_done, n + 1)
                link(dve.tensor_tensor(ssum[i], ssum[i], ses[i], ALU.add))
                link(dve.reciprocal(ssum[i], ssum[i]))
                dve.tensor_tensor(Pm, Pm, ssum[i].unsqueeze(2).broadcast_to([P, NQ, P]), ALU.mult).then_inc(pn_done, 1)

            def copy_turned(l, b):
                n = TT * l + b
                dve.wait_ge(pt_done, n + 1)
                if b > 0:
                    dve.wait_ge(o_done, n)
                dve.tensor_copy(PT[:, 4:8, :], bank[1][:, :].rearrange("p (h q) -> p h q", h=4)).then_inc(pt_dve, 1)

            def gmlp(l, m):
                dve.wait_ge(gm_done, 2 * l + m + 1)
                bc = bsp[:, m, :].unsqueeze(1).broadcast_to([P, TT, P])
                ps = bank[3][:, :].rearrange("p (j i) -> p j i", j=TT)
                link(dve.tensor_tensor(cat[:, 6 + m, :].rearrange("p (j i) -> p j i", j=TT), ps, bc, ALU.add))
                dve.tensor_tensor(cat[:, 6 + m, :], cat[:, 6 + m, :], u[:, m, :], ALU.mult).then_inc(gm_cat, 1)

            def norm_in(l, j, ffn):
                q = 2 * l + ffn
                if ffn:
                    dve.wait_ge(y_in[j % 2], 16 * (2 * l + j // 2 + 1))
                    link(dve.scalar_tensor_tensor(xtok[:, j, :], xtok[:, j, :], ALPHA, ycomb[j % 2][:, 0, :],
                                                  ALU.mult, ALU.add))
                    link(dve.tensor_tensor(xtok[:, j, :], xtok[:, j, :], ycomb[j % 2][:, 1, :], ALU.add))
                    dve.sem_inc(y_added, 1)
                else:
                    dve.wait_ge(xb_done, TT * l + j + 1)
                    dve.wait_ge(op_done, TT * l + j + 1)
                    for n in range(2):
                        x = xtok[:, j, 512 * n:512 * n + 512]
                        link(dve.tensor_tensor(x, x, bank[2 * (j % 2) + n][:, :], ALU.add))
                    dve.sem_inc(op_used, 1)
                norm_stats([xtok[:, j, 0:512], xtok[:, j, 512:1024]], j, 2)
                link(dve.tensor_scalar(ve[:, j:j + 1], mv[:, 2 * j + 1:2 * j + 2], EPS, None, ALU.add))
                dve.sem_inc(ln_var, 1)

            def norm_out(l, j, ffn):
                q = 2 * l + ffn
                dve.wait_ge(ln_rstd, TT * q + j + 1)
                dve.tensor_scalar(xtok[:, j, :], xtok[:, j, :], mv[:, 2 * j:2 * j + 1], rstd[:, j:j + 1],
                                  ALU.subtract, ALU.mult).then_inc(ln_norm, 1)

            def norm(l, ffn):
                for j in range(TT):
                    norm_in(l, j, ffn)
                    if j >= 1:
                        norm_out(l, j - 1, ffn)
                norm_out(l, TT - 1, ffn)

            def bc3(x, n):
                return x.unsqueeze(2).broadcast_to([P, x.shape[1], n])

            def route(l):
                dve.wait_ge(lg_done, l + 1)
                ps = bank[0][:, 0:TT * E].rearrange("p (j e) -> p j e", j=TT)
                top, tot, s1, s2, m1, m2 = r4
                link(dve.tensor_reduce(top, ps, AX.X, ALU.max))
                link(dve.tensor_tensor(lg, ps, bc3(top, E), ALU.subtract))
                dve.sem_inc(rt_sub, 1)
                dve.wait_ge(rt_exp, l + 1)
                link(dve.tensor_reduce(tot, ex, AX.X, ALU.add))
                link(dve.reciprocal(tot, tot))
                link(dve.tensor_tensor(ex, ex, bc3(tot, E), ALU.mult))
                rb = col[:, C_RB:C_RB + E].unsqueeze(1).broadcast_to([P, TT, E])
                link(dve.tensor_tensor(sel, ex, rb, ALU.add))
                s4 = sel.rearrange("p j (g m) -> p (j g) m", g=G)
                dve.tensor_tensor(pr[:, :, 0:3], s4[:, :, 0:3], s4[:, :, 1:4], ALU.add)
                dve.tensor_tensor(pr[:, :, 3:5], s4[:, :, 0:2], s4[:, :, 2:4], ALU.add)
                link(dve.tensor_tensor(pr[:, :, 5:6], s4[:, :, 0:1], s4[:, :, 3:4], ALU.add))
                link(dve.tensor_reduce(gsc.rearrange("p j g -> p (j g)"), pr, AX.X, ALU.max))

                def first_max(hot, vals, keys, width, m):
                    link(dve.tensor_reduce(m, vals, AX.X, ALU.max))
                    link(dve.tensor_tensor(hot, vals, bc3(m, width), ALU.is_equal))
                    kb = keys.unsqueeze(1).broadcast_to([P, TT, width])
                    link(dve.tensor_tensor(hot, hot, kb, ALU.mult))
                    link(dve.tensor_reduce(m, hot, AX.X, ALU.max))
                    link(dve.tensor_tensor(hot, hot, bc3(m, width), ALU.is_equal))

                first_max(ing, gsc, cst[:, K_KG:K_KG + G], G, m1)
                inb = ing.rearrange("p j g -> p (j g)").unsqueeze(2).broadcast_to([P, TT * G, EG])
                link(dve.tensor_tensor(smk.rearrange("p j (g m) -> p (j g) m", g=G), s4, inb, ALU.mult))
                link(dve.tensor_scalar(gkey, ing, 1e30, -1e30, ALU.mult, ALU.add))
                gb = gkey.rearrange("p j g -> p (j g)").unsqueeze(2).broadcast_to([P, TT * G, EG])
                s4m = smk.rearrange("p j (g m) -> p (j g) m", g=G)
                link(dve.tensor_tensor(s4m, s4m, gb, ALU.add))
                ke = cst[:, K_KE:K_KE + E]
                first_max(oh1, smk, ke, E, m1)
                link(dve.scalar_tensor_tensor(smk, oh1, -3e38, smk, ALU.mult, ALU.add))
                first_max(oh2, smk, ke, E, m2)
                link(dve.tensor_tensor(selb[:, :, :], oh1, oh2, ALU.add))
                dve.sem_inc(rt_sel, 1)

                def pick(out, vals, hot):
                    link(dve.tensor_tensor(kk, vals, hot, ALU.mult))
                    link(dve.tensor_reduce(out, kk, AX.X, ALU.add))

                pick(s1, ex, oh1)
                pick(s2, ex, oh2)
                link(dve.tensor_tensor(m1, s1, s2, ALU.add))
                link(dve.reciprocal(m1, m1))
                dve.tensor_tensor(gt[:, 0:TT], s1, m1, ALU.mult)
                link(dve.tensor_tensor(gt[:, TT:2 * TT], s2, m1, ALU.mult))
                dve.wait_ge(rk_done, l + 1)
                cnt = bank[1][:, TT * E:TT * E + E]
                link(dve.tensor_scalar(nch, cnt, float(P), 1.0, ALU.is_gt, ALU.add))
                for n in (2, 3):
                    link(dve.scalar_tensor_tensor(nch, cnt, float(P * n), nch, ALU.is_gt, ALU.add))
                if l == 0:
                    link(dve.memset(startf[:, 0, 0:1], 0.0))
                else:
                    link(dve.tensor_copy(startf[:, l, 0:1], startf[:, l - 1, E:E + 1]))
                link(dve.memset(zero16, 0.0))
                link(dve.tensor_tensor_scan(startf[:, l, 1:E + 1], nch, zero16, startf[:, l, 0:1], ALU.add, ALU.add))
                rank = bank[1][:, 0:TT * E].rearrange("p (j e) -> p j e", j=TT)
                stb = startf[:, l, 0:E].unsqueeze(1).broadcast_to([P, TT, E])
                for i, hot in enumerate((oh1, oh2)):
                    pick(rk[:, TT * i:TT * i + TT], rank, hot)
                    pick(stc[:, TT * i:TT * i + TT], stb, hot)
                link(dve.tensor_scalar(ovf, rk, float(P), None, ALU.is_ge))
                for n in (2, 3):
                    link(dve.scalar_tensor_tensor(ovf, rk, float(P * n), ovf, ALU.is_ge, ALU.add))
                link(dve.tensor_tensor(stc, stc, ovf, ALU.add))
                link(dve.scalar_tensor_tensor(rk, ovf, -float(P), rk, ALU.mult, ALU.add))
                iota = cst[:, K_IOTA:K_IOTA + P]
                dve.tensor_tensor(hotA, iota.unsqueeze(1).broadcast_to([P, 8, P]), bc3(rk, P), ALU.is_equal)
                link(dve.tensor_tensor(hotB[:, :, 0, :], iota[:, 0:MAXCH].unsqueeze(1).broadcast_to([P, 8, MAXCH]),
                                       bc3(stc, MAXCH), ALU.is_equal))
                link(dve.tensor_tensor(hotB[:, :, 1, :], hotB[:, :, 0, :], bc3(gt, MAXCH), ALU.mult))
                link(dve.tensor_tensor(hotB[:, :, 0, :], hotB[:, :, 0, :], bc3(cst[:, K_DEST:K_DEST + 8], MAXCH),
                                       ALU.mult))
                dve.sem_inc(rt_hot, 1)
                dve.wait_ge(tab_done, l + 1)
                link(dve.tensor_scalar(tabf, bank[2][:, 0:MAXCH], float(OOB), None, ALU.add))
                dve.tensor_copy(gatef[:, :], bank[2][:, MAXCH:2 * MAXCH])
                dve.tensor_copy(dsti[:, :], tabf)
                dve.tensor_copy(starti[:, l * (E + 1):(l + 1) * (E + 1)], startf[:, l, :])
                link(dve.tensor_scalar(tab2, tabf, float(T), -float(T), ALU.is_ge, ALU.mult))
                link(dve.tensor_tensor(toki[:, :], tabf, tab2, ALU.add))
                dve.sem_inc(tab_set, 1)

            def copy_gathered(c, l):
                dve.wait_ge(xg_turned, c + (l + 1))
                dve.tensor_copy(xgT[:, 4:8, :], bank[3][:, :].rearrange("p (k t) -> p k t", k=4)).then_inc(xgT_dve, 1)

            dve.memset(onesc[:, :], 1.0 / CONV).then_inc(ones_set, 1)
            dve.memset(onesb[:, :], 1.0).then_inc(ones_set, 1)
            dve.memset(wsT[64:P, :, 0:64], 0.0).then_inc(ones_set, 1)
            link(dve.memset(eps, EPS))
            link(dve.memset(mhalf, -0.5))
            for l in range(DEPTH):
                dve.wait_ge(col_in, 16 * (l + 1))
                conv(l)
                if l == 0:
                    dve.wait_ge(const_in, 32)
                    dve.tensor_copy(utri[:, :], cst[:, K_UTRI:K_UTRI + P]).then_inc(ones_set, 1)
                for m in range(4):
                    rope(l, m, qr[:, m, :])
                tokens(l, 0)
                tokens(l, 1)
                rope(l, 4, kr)
                dve.wait_ge(mean_done, l + 1)
                for m in range(2):
                    dve.tensor_tensor(cat[:, m, :], cat[:, m, :], bank[5][:, :], ALU.subtract).then_inc(cen_set, 1)
                dve.wait_ge(cen_set, 2 * (l + 1))
                for g in range(2):
                    link(dve.memset(bank[4 + g][0:64, :].rearrange("p (h k) -> p h k", h=4)[:, :, 0:64], -1e30))
                dve.sem_inc(mask_set, 1)
                tokens(l, 2)
                tokens(l, 3)
                for j in range(TT):
                    dve.wait_ge(gv_act, TT * l + j + 1)
                    norm_stats([gv[:, j, :]], j, 1)
                link(dve.tensor_scalar(ve, mv.rearrange("p (j s) -> p s j", s=2)[:, 1, :], EPS, None, ALU.add))
                dve.sem_inc(gvar_set, 1)
                softmax_max(l, 0)
                dve.wait_ge(grstd_set, l + 1)
                for j in range(TT):
                    link(dve.tensor_scalar(gv[:, j, :], gv[:, j, :], mv[:, 2 * j:2 * j + 1], rstd[:, j:j + 1],
                                           ALU.subtract, ALU.mult))
                dve.sem_inc(gvh_set, 1)
                softmax_max(l, 1)
                dve.wait_ge(sd_set, l + 1)
                link(dve.reciprocal(tmp[:, 0:T], tmp[:, 0:T]))
                for m in range(2):
                    dve.tensor_tensor(cat[:, m, :], cat[:, m, :], tmp[:, 0:T], ALU.mult).then_inc(conv_norm, 1)
                softmax_norm(l, 0)
                copy_turned(l, 0)
                softmax_max(l, 2)
                softmax_norm(l, 1)
                copy_turned(l, 1)
                softmax_norm_after = [2, 3]
                gmlp(l, 0)
                gmlp(l, 1)
                softmax_max(l, 3)
                for b in softmax_norm_after:
                    softmax_norm(l, b)
                    copy_turned(l, b)
                norm(l, 0)
                route(l)
                copy_gathered(first_chunk(dve, l, 0), l)
                with dve.Fori(first_chunk(dve, l, 0), first_chunk(dve, l, E)) as c:
                    dve.wait_ge(up_used, c + 1)
                    dve.wait_ge(sg_set, c + 1)
                    dve.wait_ge(he_turned, c)
                    dve.tensor_tensor(he, bank[1][:, :], sg, ALU.mult).then_inc(he_set, 1)
                    copy_gathered(c + 1, l)
                    dve.wait_ge(down_used, c + 1)
                    dve.wait_ge(cur_set, c + 1)
                    dve.wait_ge(scattered, c * 16)
                    dve.tensor_scalar(ysb[:, 512:1024], bank[6][:, :], gate_cur[:, :], None, ALU.mult)\
                       .then_inc(y_dve, 1)
                dve.wait_ge(rows_in, 32 * (l + 1))
                norm(l, 1)

        @block.gpsimd
        def _(pool):
            chain = [0]

            def link(x):
                chain[0] += 1
                x.then_inc(pool_chain, 1)
                pool.wait_ge(pool_chain, chain[0])

            def norm(l, ffn):
                q = 2 * l + ffn
                gain = rows3[:, 0 if ffn else 1, :]
                offset = rows3[:, 1 if ffn else 2, :]
                for j in range(TT):
                    pool.wait_ge(ln_var, TT * q + j + 1)
                    pool.tensor_tensor(rstd[:, j:j + 1], ve[:, j:j + 1], mhalf[:, 0:1], ALU.pow).then_inc(ln_rstd, 1)
                    pool.wait_ge(ln_norm, TT * q + j + 1)
                    link(pool.tensor_tensor(xtok[:, j, :], xtok[:, j, :], gain, ALU.mult))
                    link(pool.tensor_tensor(xtok[:, j, :], xtok[:, j, :], offset, ALU.add))
                    pool.sem_inc(ln_out, 1)
                    rows = slice(P * j, P * j + P)
                    if not ffn:
                        pool.dma_start(x1d[l][rows, :], xtok[:, j, :]).then_inc(x1_stored, 16)
                    elif l == DEPTH - 1:
                        pool.dma_start(a["out"][rows, :], xtok[:, j, :]).then_inc(out_stored, 16)

            def gather(c, l):
                pool.tensor_copy(gather_idx[:, :], toki[:, bass.ds(c, 1)]).then_inc(idx_set, 1)
                pool.wait_ge(idx_set, c + (l + 1))
                pool.sem_inc(gather_sent, 1)
                pool.indirect_dma_start(xg, None, x1d[l], bass.IndirectOffsetOnAxis(ap=gather_idx[:, :], axis=0),
                                        bounds_check=T - 1, oob_is_err=False).then_inc(gathered, 16)

            for l in range(DEPTH):
                if l > 0:
                    pool.wait_ge(o_done, TT * l)
                link(pool.memset(vmem[0:64, 1, 0, :], 0.0))
                for j in range(TT):
                    pool.wait_ge(v_set, TT * l + j + 1)
                    if j == 1 or j == 3:
                        pool.dma_start(vmem[64:128, 1, j - 1:j + 1, :], vmem[0:64, 0, j - 1:j + 1, :])\
                            .then_inc(voff_in, 16)
                        if j == 1:
                            pool.dma_start(vmem[0:64, 1, 1:3, :], vmem[64:128, 0, 0:2, :]).then_inc(voff_in, 16)
                        else:
                            pool.dma_start(vmem[0:64, 1, 3:4, :], vmem[64:128, 0, 2:3, :]).then_inc(voff_in, 16)
                pool.wait_ge(gvar_set, l + 1)
                pool.tensor_tensor(rstd, ve, mhalf, ALU.pow).then_inc(grstd_set, 1)
                pool.wait_ge(gvh_set, l + 1)
                for i, op in ((0, ALU.mult), (1, ALU.add)):
                    o = P + GM * (i + 1)
                    link(pool.tensor_tensor(gv, gv, rowm[:, o:o + GM].unsqueeze(1).broadcast_to([P, TT, GM]), op))
                pool.sem_inc(gvn_set, 1)
                if l == 0:
                    pool.wait_ge(xtok_in, 16)
                for j in range(TT):
                    link(pool.tensor_scalar(xtok[:, j, :], xtok[:, j, :], ALPHA, None, ALU.mult))
                pool.wait_ge(rows_in, 32 * l + 16)
                for j in range(TT):
                    link(pool.tensor_tensor(xtok[:, j, :], xtok[:, j, :], rows3[:, 0, :], ALU.add))
                    pool.sem_inc(xb_done, 1)
                norm(l, 0)
                pool.wait_ge(op_done, TT * (l + 1))
                link(pool.memset(xg, 0.0))
                pool.wait_ge(x1_stored, 16 * TT * (l + 1))
                pool.wait_ge(tab_set, l + 1)
                gather(first_chunk(pool, l, 0), l)
                with pool.Fori(first_chunk(pool, l, 0), first_chunk(pool, l, E)) as c:
                    pool.wait_ge(xg_turned, c + (l + 1))
                    pool.wait_ge(gathered, (c + (l + 1)) * 16)
                    gather(c + 1, l)
                    pool.wait_ge(y_act, c)
                    pool.wait_ge(y_dve, c)
                    pool.wait_ge(scattered, c * 16)
                    pool.tensor_copy(gate_cur[:, :], gatef[:, bass.ds(c, 1)]).then_inc(cur_set, 1)
                    pool.tensor_copy(scatter_idx[:, :], dsti[:, bass.ds(c, 1)]).then_inc(dst_set, 1)
                    pool.wait_ge(dst_set, c + 1)
                    pool.wait_ge(y_act, c + 1)
                    pool.wait_ge(y_dve, c + 1)
                    pool.sem_inc(scatter_sent, 1)
                    pool.indirect_dma_start(yd[l], bass.IndirectOffsetOnAxis(ap=scatter_idx[:, :], axis=0), ysb, None,
                                            bounds_check=2 * T - 1, oob_is_err=False).then_inc(scattered, 16)
                norm(l, 1)
            pool.wait_ge(out_stored, 16 * TT)


def constants():
    c = np.zeros((P, NCONST), np.float32)
    p = np.arange(P)
    c[:, K_ID:K_ID + P] = np.eye(P)
    half = ROPE // 2
    for g in range(2):
        for i in range(half):
            c[64 * g + i + half, K_PERM + 64 * g + i] = -1.0
            c[64 * g + i, K_PERM + 64 * g + i + half] = 1.0
    c[:, K_UTRI:K_UTRI + P] = p[:, None] < p[None, :]
    c[:, K_IOTA:K_IOTA + P] = p[None, :]
    c[:, K_KE:K_KE + E] = E - np.arange(E)
    c[:, K_KG:K_KG + G] = G - np.arange(G)
    for r in range(2):
        for j in range(TT):
            c[:, K_DEST + TT * r + j] = r * T + P * j + p - OOB
    freq = np.power(np.float32(THETA), -np.arange(half, dtype=np.float32) / np.float32(half)).astype(np.float32)
    ang = (np.arange(T, dtype=np.float32)[None, :] * freq[:, None]).astype(np.float32)
    c[:, K_COS:K_COS + T] = 1.0
    for g in range(2):
        for i in range(2):
            rows = slice(64 * g + half * i, 64 * g + half * (i + 1))
            c[rows, K_COS:K_COS + T] = np.cos(ang)
            c[rows, K_SIN:K_SIN + T] = np.sin(ang)
    return c


def kernel(**inputs):
    from concourse import bacc
    from concourse.bass_utils import run_bass_kernel_spmd

    x = {n: np.asarray(v) for n, v in inputs.items()}
    order = np.arange(NQ).reshape(2, 4).T.reshape(-1)
    qcols = (order[:, None] * HD + np.arange(HD)).reshape(-1)
    o_q, o_k, o_v, o_g = 2 * CONV, 2 * CONV + NQ * HD, 2 * CONV + (NQ + NKV) * HD, 2 * CONV + (NQ + 2 * NKV) * HD
    cols = np.concatenate([np.arange(CONV, 2 * CONV), np.arange(CONV), o_q + qcols, np.arange(o_k, o_g),
                           np.arange(o_g + GM, o_g + 2 * GM), np.arange(o_g, o_g + GM)])
    rows = np.concatenate([np.arange(CONV), CONV + qcols, np.arange(CONV + NQ * HD, D)])
    w_in = np.ascontiguousarray(x["w_in"][:, :, cols])
    b_in = x["b_in"][:, cols]

    def columns(v):
        return v.reshape(DEPTH, -1, P).transpose(0, 2, 1)

    conv_w = x["conv_w"].transpose(0, 2, 1).reshape(DEPTH, 2, P, TAPS).transpose(0, 2, 1, 3).reshape(DEPTH, P, 2 * TAPS)
    percol = np.concatenate([
        columns(b_in), conv_w, columns(x["conv_b"]), columns(x["conv_ln_g"]), columns(x["conv_ln_b"]),
        np.broadcast_to(x["attn_sinks"][:, None, :], (DEPTH, P, NQ)),
        np.broadcast_to(x["router_bias"][None, None, :], (DEPTH, P, E))], axis=2)
    v_at = 2 * CONV + NQ * HD + NKV * HD
    arrays = {
        "x": x["x"].reshape(T, D), "x_t": np.ascontiguousarray(x["x"].reshape(T, D).T),
        "w_in": w_in, "w_out": np.ascontiguousarray(x["w_out"][:, rows, :]), "cols": np.ascontiguousarray(percol),
        "rowm": np.concatenate([b_in[:, v_at:v_at + NKV * HD + GM], x["gmlp_ln_g"], x["gmlp_ln_b"]], axis=1),
        "ws_t": np.ascontiguousarray(x["gmlp_w_s"].transpose(0, 1, 3, 2)), "gmlp_b_s": x["gmlp_b_s"],
        "rows_mix": np.stack([x["b_out"], x["ln_mix_g"], x["ln_mix_b"]], axis=1),
        "rows_ffn": np.stack([x["ln_ffn_g"], x["ln_ffn_b"]], axis=1),
        "w_router": x["w_router"], "const": constants(),
        "exp_w_gate": x["exp_w_gate"].reshape(DEPTH * E, D, FE), "exp_w_up": x["exp_w_up"].reshape(DEPTH * E, D, FE),
        "exp_w_down": x["exp_w_down"].reshape(DEPTH * E, FE, D),
    }
    nc = bacc.Bacc("TRN2", target_bir_lowering=False, num_devices=1)
    a = {n: nc.dram_tensor(f"in_{n}", v.shape, mybir.dt.from_np(v.dtype), kind="ExternalInput").ap()
         for n, v in arrays.items()}
    a["out"] = nc.dram_tensor("out_x", (T, D), F32, kind="ExternalOutput").ap()
    build(nc, a)
    r = run_bass_kernel_spmd(nc, [{f"in_{n}": v for n, v in arrays.items()}], core_ids=[0])
    return r.results[0]["out_x"].reshape(1, T, D)
```

```python
from contextlib import ExitStack

import numpy as np

import concourse.bass as bass
from concourse import mybir

F32 = mybir.dt.float32
BF16 = mybir.dt.bfloat16
I32 = mybir.dt.int32
F32R = mybir.dt.float32r
ALU = mybir.AluOpType
ACT = mybir.ActivationFunctionType
AX = mybir.AxisListType

P = 128
D = 1024
KD = D // P
T = 512
TT = T // P
DEPTH = 2
CONV = 256
TAPS = 31
HD = 64
NQ = 8
NKV = 2
ROPE = HD // 4
THETA = 500000.0
GM = 256
GH = 4
D_IN = 2 * CONV + NQ * HD + 2 * NKV * HD + 2 * GM
E = 16
G = 4
EG = E // G
FE = D // 2
KF = FE // P
EPS = 1e-5
ALPHA = (2 * DEPTH) ** 0.25
PIECE = 256
NPIECE = D_IN // PIECE
MAXCH = 48
OOB = 4096
C_BIN, C_CW, C_CB, C_CG, C_CLB, C_SINK, C_RB = 0, 14, 76, 78, 80, 82, 90
NCOL = 106
K_ID, K_IOTA, K_KE, K_KG, K_DEST = 0, 128, 256, 272, 276
NCONST = 284
M_COS, M_SIN, M_PERM, M_UTRI = 0, T, 2 * T, 2 * T + P
NMIX = 2 * T + 2 * P
PROJ = 14
PROJ_ACT = (0, 2, 4, 5, 6, 7, 8, 9, 10, 11, 12, 13)
PROJ_DVE = (1, 3)
PIECES = NPIECE + 4
PIECE_FREE = {3: 3, 4: 4, 5: 6, 6: 8, 7: 10, 8: 12, 9: 14}
HALVES = 6
SLOTS = 3
POOL_HALF = 5


def build(nc, a):
    ctx = ExitStack()
    with ctx:
        def sem(name):
            return ctx.enter_context(nc.semaphore(name))

        def sb(name, shape, dt=F32):
            return ctx.enter_context(nc.sbuf_tensor(name, shape, dt))

        slot = [[sb(f"w_{n}{r}", [P, 4096]) for n in ("gate", "up", "down")] for r in range(2)]
        wh = [sb(f"wh{i}", [P, 2048], F32R) for i in range(SLOTS)]
        wl = [sb(f"wl{i}", [P, 2048], F32R) for i in range(SLOTS)]
        xTh = sb("xTh", [P, KD * T], F32R)
        xTl = sb("xTl", [P, KD * T], F32R)
        xtok = sb("xtok", [P, TT, D])
        xparts = [x[:, :].rearrange("p (k t) -> p k t", k=KD) for x in (xTh, xTl)]
        xgT = [x[:, 0:1024].rearrange("p (k t) -> p k t", k=KD) for x in (xTh, xTl)]
        heT = [x[:, 1024:1536].rearrange("p (k t) -> p k t", k=KF) for x in (xTh, xTl)]
        moemem = sb("moemem", [P, 2560])
        xg, ysb, sg = moemem[:, 0:1024], moemem[:, 1024:2048], moemem[:, 2048:2560]

        qr = slot[0][0][:, 0:2048].rearrange("p (m t) -> p m t", m=4)
        gv = slot[0][0][:, 2048:3072].rearrange("p (j c) -> p j c", j=TT)
        kr = slot[0][0][:, 3072:3584]
        rows3 = slot[0][0][:, 0:3072].rearrange("p (r n) -> p r n", r=3)
        cv = slot[0][1][:, 0:1024].rearrange("p (m t) -> p m t", m=2)
        gmr = slot[0][1][:, 1024:2048].rearrange("p (m t) -> p m t", m=2)
        vT = slot[0][1][:, 2048:2560]
        gvT = slot[0][1][:, 2560:3584].rearrange("p (m t) -> p m t", m=2)
        ycomb = [slot[0][1][:, 2048 * i:2048 * i + 2048].rearrange("p (r n) -> p r n", r=2) for i in range(2)]
        glu = slot[0][2][:, 0:2 * (T + TAPS - 1)].rearrange("p (m t) -> p m t", m=2)
        tmp = slot[0][2][:, 1084:2108]
        Pm = [x.rearrange("p (h k) -> p h k", h=NQ) for x in (slot[0][2][:, 0:1024], tmp)]
        u = slot[0][2][:, 2108:3132].rearrange("p (m t) -> p m t", m=2)
        wraw = [slot[1][0][:, 2048 * i:2048 * i + 2048] for i in range(2)]
        xraw = slot[1][1][:, :].rearrange("p (k t) -> p k t", k=KD)
        mixc = slot[1][2][:, 0:NMIX]
        PT = slot[1][2][:, 0:2 * T].rearrange("p (h q) -> p h q", h=NQ)
        cosT, sinT = mixc[:, M_COS:M_COS + T], mixc[:, M_SIN:M_SIN + T]
        perm = mixc[:, M_PERM:M_PERM + P]
        vmem = slot[1][2][:, 1280:2304].rearrange("p (o j c) -> p o j c", o=2, j=TT)
        wsT = slot[1][2][:, 2304:2816].rearrange("p (h i) -> p h i", h=GH)
        bsp = slot[1][2][:, 2816:3072].rearrange("p (m i) -> p m i", m=2)
        rowm = slot[1][2][:, 3072:3584]
        scr = slot[1][2]

        cst = sb("cst", [P, NCONST])
        col = sb("col", [P, NCOL])
        wr = sb("wr", [P, KD, E])
        ident = cst[:, K_ID:K_ID + P]
        onesc = sb("onesc", [P, P])
        onesb = sb("onesb", [P, P], BF16)
        utri = sb("utri", [P, P], BF16)
        selb = sb("selb", [P, TT, E], BF16)
        small = sb("small", [P, 112])
        startf = sb("startf", [P, DEPTH, E + 1])
        starti = sb("starti", [P, DEPTH * (E + 1)], I32)
        toki = sb("toki", [P, MAXCH], I32)
        dsti = sb("dsti", [P, MAXCH], I32)
        gatef = sb("gatef", [P, MAXCH])
        gather_idx = sb("gather_idx", [P, 1], I32)
        scatter_idx = sb("scatter_idx", [P, 1], I32)
        gate_cur = sb("gate_cur", [P, 1])
        idle = sb("idle", [P, 1])
        eps = small[:, 0:1]
        mhalf = small[:, 1:5]
        bn6 = small[:, 8:20]
        mv = small[:, 20:28]
        ve = small[:, 28:32]
        rstd = small[:, 32:36]
        smax, snmax, ses, ssum = ([small[:, 48 + 32 * b + 8 * i:56 + 32 * b + 8 * i] for b in range(2)]
                                  for i in range(4))
        lg, ex, sel, smk, key, oh1, oh2, kk = (
            scr[:, 64 * i:64 * i + 64].rearrange("p (j e) -> p j e", j=TT) for i in range(8))
        pr = scr[:, 512:608].rearrange("p (g m) -> p g m", m=6)
        gsc, gkey, ing = (scr[:, 608 + 16 * i:624 + 16 * i].rearrange("p (j g) -> p j g", j=TT) for i in range(3))
        r4 = [scr[:, 656 + 4 * i:660 + 4 * i] for i in range(6)]
        nch = scr[:, 680:696]
        zero16 = scr[:, 696:712]
        rk = scr[:, 712:720]
        stc = scr[:, 720:728]
        ovf = scr[:, 728:736]
        gt = scr[:, 736:744]
        tabf = scr[:, 752:752 + MAXCH]
        tab2 = scr[:, 800:800 + MAXCH]
        hotA = scr[:, 1024:2048].rearrange("p (q s) -> p q s", q=8)
        lgT = scr[0:E, 1024:1536]
        hotB = scr[:, 2048:2048 + 8 * 2 * MAXCH].rearrange("p (q v c) -> p q v c", q=8, v=2)
        wrp = [x[:, 0:KD * E].rearrange("p (k e) -> p k e", k=KD) for x in (wh[0], wl[0])]

        bank = [ctx.enter_context(nc.psum_tensor(f"bank{i}", [P, 512], F32)) for i in range(8)]

        x1d = [nc.dram_tensor(f"x1_rows{l}", [T, D], F32, kind="Internal").ap() for l in range(DEPTH)]
        yd = [nc.dram_tensor(f"y_rows{l}", [2 * T, D], F32, kind="Internal").ap() for l in range(DEPTH)]

        const_in, ones_set = sem("const_in"), sem("ones_set")
        col_in, mixc_in, row_in, gm_in = sem("col_in"), sem("mixc_in"), sem("row_in"), sem("gm_in")
        xT_in = [sem(f"xT_in{i}") for i in range(4)]
        xtok_in, wr_in = sem("xtok_in"), sem("wr_in")
        wraw_in = [sem(f"wraw_in{i}") for i in range(2)]
        rows_in = sem("rows_in")
        wexp_in = [[sem(f"{n}_in{r}") for n in ("gate", "up", "down")] for r in range(2)]
        dve_chain, pool_chain = sem("dve_chain"), sem("pool_chain")
        xT_high, xT_low = sem("xT_high"), sem("xT_low")
        piece_high, piece_low, last_low = sem("piece_high"), sem("piece_low"), sem("last_low")
        proj_done = sem("proj_done")
        proj_act, proj_dve = sem("proj_act"), sem("proj_dve")
        sig_set, glu_read, rot_done, rot_used = sem("sig_set"), sem("glu_read"), sem("rot_done"), sem("rot_used")
        conv_acc, mean_done, cen_set, sq_set, var_done, sd_set, conv_norm, conv_raw, conv_high, conv_low = (
            sem(n) for n in ("conv_acc", "mean_done", "cen_set", "sq_set", "var_done", "sd_set", "conv_norm",
                             "conv_raw", "conv_high", "conv_low"))
        v_turned, v_set, voff_in = sem("v_turned"), sem("v_set"), sem("voff_in")
        gv_turned, gvar_set, grstd_set, gvh_set, gvn_set, gm_done, gm_raw, gm_high, gm_low = (
            sem(n) for n in ("gv_turned", "gvar_set", "grstd_set", "gvh_set", "gvn_set", "gm_done",
                             "gm_raw", "gm_high", "gm_low"))
        ws_zeroed = sem("ws_zeroed")
        mask_set, s_done, s_max, p_done, pn_done, pt_done, pt_act, pt_dve, o_done, o_high, o_low = (
            sem(n) for n in ("mask_set", "s_done", "s_max", "p_done", "pn_done", "pt_done", "pt_act", "pt_dve",
                             "o_done", "o_high", "o_low"))
        xb_done, op_quarter, op_done = sem("xb_done"), sem("op_quarter"), sem("op_done")
        ln_var, ln_rstd, ln_norm, ln_scaled, ln_out = (
            sem(n) for n in ("ln_var", "ln_rstd", "ln_norm", "ln_scaled", "ln_out"))
        x1_stored, tr_done, tr_high, tr_low = sem("x1_stored"), sem("tr_done"), sem("tr_high"), sem("tr_low")
        wr_high, wr_low = sem("wr_high"), sem("wr_low")
        lgT_done, lgT_set = sem("lgT_done"), sem("lgT_set")
        lg_done, rt_sub, rt_exp, rt_sel, rk_done, rt_hot, tab_done, tab_set = (
            sem(n) for n in ("lg_done", "rt_sub", "rt_exp", "rt_sel", "rk_done", "rt_hot", "tab_done", "tab_set"))
        idx_set, gathered, dst_set = sem("idx_set"), sem("gathered"), sem("dst_set")
        gather_sent, scatter_sent = sem("gather_sent"), sem("scatter_sent")
        cur_set, scattered = sem("cur_set"), sem("scattered")
        xg_turned, xgT_high, xgT_low = sem("xg_turned"), sem("xgT_high"), sem("xgT_low")
        half_high, half_low, half_low_pool, half_used = (
            sem(n) for n in ("half_high", "half_low", "half_low_pool", "half_used"))
        split_done = [sem(f"{n}_split") for n in ("gate", "up", "down")]
        he_first = sem("he_first")
        sg_set, he_set, he_turned, heT_high, heT_low, y_set = (
            sem(n) for n in ("sg_set", "he_set", "he_turned", "heT_high", "heT_low", "y_set"))
        y_in = [sem(f"y_in{i}") for i in range(2)]
        y_summed = sem("y_summed")
        y_added, out_stored = sem("y_added"), sem("out_stored")

        block = ctx.enter_context(nc.Block())

        def first_chunk(eng, l, e):
            return eng.value_load(starti[0:1, bass.ds(l * (E + 1) + e, 1)], min_val=0, max_val=MAXCH - 1)


        def chunk_loops(eng, l, body):
            with eng.Fori(0, E // 2) as pair:
                starts = [first_chunk(eng, l, 2 * pair + r) for r in range(2)]
                for r in range(2):
                    if r == 1:
                        starts.append(first_chunk(eng, l, 2 * pair + 2))
                    with eng.Fori(starts[r], starts[r + 1]) as c:
                        body(c, pair, r)

        def halves(i):
            return i // 2, slice(2048 * (i % 2), 2048 * (i % 2) + 2048), i % SLOTS

        def halves_done(c, piece, back=0):
            return c * HALVES + (2 * (piece + 1) + SLOTS - HALVES * back)

        def lows_done(c, i):
            return c * (HALVES - 1) + (i + 1 if i < POOL_HALF else i)

        @block.sync
        def _(sp):
            def mix_params(l):
                sp.dma_start(mixc, a["mixc"]).then_inc(mixc_in, 16)
                sp.dma_start(rowm, a["rowm"][l].partition_broadcast(P)).then_inc(row_in, 16)
                ws = a["ws_t"][l].rearrange("h j i -> j h i")
                sp.dma_start(wsT[0:64, :, :], ws[0:64, :, :]).then_inc(gm_in, 16)
                sp.dma_start(wsT[64:P, :, 64:P], ws[64:P, :, 64:P]).then_inc(gm_in, 16)
                for m in range(2):
                    for g in range(2):
                        sp.dma_start(bsp[64 * g:64 * g + 64, m, :],
                                     a["gmlp_b_s"][l, 2 * m + g].partition_broadcast(64)).then_inc(gm_in, 16)

            def load_piece(l, q):
                n = PIECES * l + q
                if q < NPIECE:
                    src = a["w_in"][l, :, q * PIECE:(q + 1) * PIECE].rearrange("(k p) n -> p k n", p=P)
                else:
                    h, k = (q - NPIECE) // 2, (q - NPIECE) % 2
                    src = a["w_out"][l, 512 * k:512 * k + 512, 512 * h:512 * h + 512].rearrange("(k p) n -> p k n", p=P)
                dst = wraw[n % 2].rearrange("p (k n) -> p k n", n=src.shape[2])
                sp.dma_start(dst, src).then_inc(wraw_in[n % 2], 16)

            def load_expert(l, e, r, piece):
                w = a[("exp_w_gate", "exp_w_up", "exp_w_down")[piece]]
                k = KF if piece == 2 else KD
                sp.dma_start(slot[r][piece][:, :].rearrange("p (k n) -> p k n", k=k), w[bass.ds(l * E + e, 1), :, :]
                             .rearrange("o (k p) n -> p (o k) n", p=P)).then_inc(wexp_in[r][piece], 16)

            for l in range(DEPTH):
                if l == 0:
                    load_piece(l, 0)
                    sp.dma_start(xraw[:, 0:2, :], a["x_t"][0:256, :].rearrange("(k p) t -> p k t", p=P))\
                      .then_inc(xT_in[0], 16)
                    for i in range(1, 4):
                        sp.dma_start(xraw[:, 2 * i:2 * i + 2, :], a["x_t"][256 * i:256 * i + 256, :]
                                     .rearrange("(k p) t -> p k t", p=P)).then_inc(xT_in[i], 16)
                    sp.dma_start(col[:, :], a["cols"][l]).then_inc(col_in, 16)
                    load_piece(l, 1)
                    sp.dma_start(cst[:, :], a["const"]).then_inc(const_in, 16)
                    mix_params(l)
                else:
                    sp.dma_start(col[:, :], a["cols"][l]).then_inc(col_in, 16)
                    sp.wait_ge(split_done[0], first_chunk(sp, l - 1, E))
                    load_piece(l, 0)
                    load_piece(l, 1)
                    sp.wait_ge(split_done[2], first_chunk(sp, l - 1, E))
                    mix_params(l)
                for q in range(2, PIECES):
                    sp.wait_ge(piece_low, (PIECES - 1) * l + q - 1)
                    load_piece(l, q)
                    if q == 4 and l == 0:
                        sp.dma_start(wr[:, :, :], a["w_router"].rearrange("(k p) e -> p k e", p=P)).then_inc(wr_in, 16)
                        sp.dma_start(xtok[:, :, :], a["x"].rearrange("(j p) n -> p j n", p=P)).then_inc(xtok_in, 16)
                    if q == 4:
                        if l == 0:
                            sp.wait_ge(xT_low, 4)
                        load_expert(l, 1, 1, 1)
                sp.wait_ge(s_done, TT * (l + 1))
                sp.wait_ge(gm_done, 2 * (l + 1))
                sp.dma_start(rows3, a["rows_mix"][l].partition_broadcast(P)).then_inc(rows_in, 16)
                sp.wait_ge(pt_done, TT * (l + 1))
                sp.wait_ge(gm_raw, 2 * (l + 1))
                sp.wait_ge(conv_norm, 2 * (l + 1))
                load_expert(l, 0, 0, 2)
                sp.wait_ge(conv_low, 2 * (l + 1))
                sp.wait_ge(gm_low, 2 * (l + 1))
                load_expert(l, 0, 0, 1)
                sp.wait_ge(last_low, l + 1)
                sp.wait_ge(piece_low, (PIECES - 1) * (l + 1))
                load_expert(l, 1, 1, 0)
                sp.wait_ge(ln_out, TT * (2 * l + 1))
                load_expert(l, 0, 0, 0)
                sp.wait_ge(tab_set, l + 1)
                sp.wait_ge(xg_turned, first_chunk(sp, l, 0) + (l + 1))
                load_expert(l, 1, 1, 2)
                with sp.Fori(1, E // 2) as pair:
                    for r in range(2):
                        e = 2 * pair + r
                        done = first_chunk(sp, l, e - 1)
                        for piece in range(3):
                            sp.wait_ge(split_done[piece], done)
                            load_expert(l, e, r, piece)
                sp.wait_ge(split_done[0], first_chunk(sp, l, E - 1))
                sp.dma_start(rows3[:, 0:2, :], a["rows_ffn"][l].partition_broadcast(P)).then_inc(rows_in, 16)

        @block.tensor
        def _(pe):
            def product(out, xs, ws, first, last):
                for n, (i, k) in enumerate(((0, 0), (1, 0), (0, 1))):
                    mm = pe.matmul(out, xs[i], ws[k], start=(first and n == 0), stop=(last and n == 2))
                return mm

            def project(l):
                task = [0]

                def channels(q, m):
                    t = task[0]
                    if t >= 4 and t - 4 in PROJ_ACT:
                        pe.wait_ge(proj_act, l * len(PROJ_ACT) + PROJ_ACT.index(t - 4) + 1)
                    elif t >= 4:
                        pe.wait_ge(proj_dve, l * len(PROJ_DVE) + PROJ_DVE.index(t - 4) + 1)
                    pe.wait_ge(piece_low, (PIECES - 1) * l + q + 1)
                    n = (PIECES * l + q) % SLOTS
                    w = [x[:, :].rearrange("p (k n) -> p k n", k=KD) for x in (wh[n], wl[n])]
                    for k in range(KD):
                        if l == 0 and t == 0 and k % 2 == 0:
                            pe.wait_ge(xT_low, k // 2 + 1)
                        mm = product(bank[t % 4][:, :], [w[i][:, k, P * m:P * m + P] for i in range(2)],
                                     [xparts[i][:, k, :] for i in range(2)], k == 0, k == KD - 1)
                    mm.then_inc(proj_done, 1)
                    task[0] += 1

                def rotate(n, src):
                    pe.wait_ge(proj_act, l * len(PROJ_ACT) + 3 + n)
                    if n == 0:
                        pe.wait_ge(mixc_in, 16 * (l + 1))
                    if n == 4:
                        pe.wait_ge(rot_used, 5 * l + 1)
                    pe.matmul(bank[4 + n % 4][:, :], perm, src, start=True, stop=True).then_inc(rot_done, 1)

                if l > 0:
                    pe.wait_ge(tr_low, 2 * TT * 2 * l)
                channels(0, 0)
                channels(1, 0)
                channels(0, 1)
                channels(1, 1)
                channels(2, 0)
                channels(2, 1)
                rotate(0, qr[:, 0, :])
                channels(3, 0)
                rotate(1, qr[:, 1, :])
                channels(3, 1)
                rotate(2, qr[:, 2, :])
                channels(4, 0)
                rotate(3, qr[:, 3, :])
                channels(4, 1)
                rotate(4, kr)
                channels(5, 0)
                if l == 0:
                    pe.wait_ge(const_in, 16)
                pe.wait_ge(proj_act, l * len(PROJ_ACT) + PROJ_ACT.index(9) + 1)
                pe.wait_ge(rot_used, 5 * l + 2)
                for j in range(TT):
                    mm = pe.transpose(bank[5][:, P * j:P * j + P], vT[:, P * j:P * j + P], ident)
                mm.then_inc(v_turned, 1)
                conv_mean(l)
                channels(5, 1)
                channels(6, 0)
                pe.wait_ge(proj_act, l * len(PROJ_ACT) + PROJ_ACT.index(11) + 1)
                for j in range(TT):
                    for m in range(2):
                        mm = pe.transpose(bank[2 + j // 2][:, GM * (j % 2) + P * m:GM * (j % 2) + P * m + P],
                                          gvT[:, m, P * j:P * j + P], ident)
                mm.then_inc(gv_turned, 1)
                conv_var(l)
                channels(6, 1)

            def conv_mean(l):
                pe.wait_ge(conv_acc, 2 * (l + 1))
                pe.wait_ge(ones_set, 3)
                for m in range(2):
                    mm = pe.matmul(bank[6][:, :], onesc[:, :], cv[:, m, :], start=(m == 0), stop=(m == 1))
                mm.then_inc(mean_done, 1)

            def conv_var(l):
                pe.wait_ge(sq_set, 2 * (l + 1))
                for m in range(2):
                    mm = pe.matmul(bank[7][:, :], onesc[:, :], tmp[:, T * m:T * m + T], start=(m == 0), stop=(m == 1))
                mm.then_inc(var_done, 1)

            def scores(l, b):
                n = TT * l + b
                if b == 0:
                    pe.wait_ge(rot_used, 5 * (l + 1))
                    pe.wait_ge(mask_set, l + 1)
                elif b == 1:
                    pe.wait_ge(sd_set, l + 1)
                    pe.wait_ge(cen_set, 2 * (l + 1))
                else:
                    pe.wait_ge(p_done, n - 1)
                for c in (2 * b, 2 * b + 1):
                    for g in range(2):
                        for m in range(4):
                            o, h = (64, 64) if c == 0 else (0, P)
                            mm = pe.matmul(bank[4 + 2 * (b % 2) + g][64 * (c % 2):64 * (c % 2) + 64, P * m + o:P * m + P],
                                           qr[64 * g:64 * g + 64, m, 64 * c:64 * c + 64],
                                           kr[64 * g:64 * g + 64, 64 * c + 64 - h:64 * c + 64], start=True, stop=True)
                mm.then_inc(s_done, 1)

            def turn_probs(l, b):
                n = TT * l + b
                pe.wait_ge(pn_done, n + 1)
                if b > 0:
                    pe.wait_ge(pt_act, n)
                    pe.wait_ge(pt_dve, n)
                else:
                    pe.wait_ge(proj_act, len(PROJ_ACT) * (l + 1))
                for h in range(NQ):
                    mm = pe.transpose(bank[h // 4][:, P * (h % 4):P * (h % 4) + P], Pm[b % 2][:, h, :], ident)
                mm.then_inc(pt_done, 1)

            def attend(l, b):
                n = TT * l + b
                pe.wait_ge(pt_act, n + 1)
                pe.wait_ge(pt_dve, n + 1)
                if b > 0:
                    pe.wait_ge(o_low, n)
                else:
                    pe.wait_ge(voff_in, 32 * (l + 1))
                    pe.wait_ge(gvh_set, l + 1)
                for c in range(2):
                    for g in range(2):
                        mm = pe.matmul(bank[2][64 * g:64 * g + 64, 256 * c:256 * c + 256],
                                       vmem[:, 1 - c, b, 64 * g:64 * g + 64],
                                       PT[:, 4 * g:4 * g + 4, 64 * c:64 * c + 64], start=True, stop=True)
                mm.then_inc(o_done, 1)

            def spatial(l, m):
                pe.wait_ge(gvn_set, l + 1)
                pe.wait_ge(gm_in, 96 * (l + 1))
                pe.wait_ge(ws_zeroed, l + 1)
                if m == 1:
                    pe.wait_ge(gm_raw, 2 * l + 1)
                for j in range(TT):
                    for g in range(2):
                        h = 2 * m + g
                        mm = pe.matmul(bank[3][64 * g:64 * g + 64, P * j:P * j + P], gv[:, j, 64 * h:64 * h + 64],
                                       wsT[:, h, :], start=True, stop=True)
                mm.then_inc(gm_done, 1)

            def project_out(l):
                for n in range(2):
                    for j in range(TT):
                        for h in range(2):
                            q = NPIECE + 2 * n + h
                            if q < PIECES - 1:
                                pe.wait_ge(piece_low, (PIECES - 1) * l + q + 1)
                            else:
                                pe.wait_ge(last_low, l + 1)
                            if n == 0 and j == 0 and h == 0:
                                pe.wait_ge(conv_low, 2 * (l + 1))
                                pe.wait_ge(gm_low, 2 * (l + 1))
                                pe.wait_ge(o_low, TT * (l + 1))
                            s = (PIECES * l + q) % SLOTS
                            w = [x[:, :].rearrange("p (k n) -> p k n", k=4) for x in (wh[s], wl[s])]
                            for k in range(4):
                                mm = product(bank[4 * n + j][:, :],
                                             [xparts[i][:, 4 * h + k, P * j:P * j + P] for i in range(2)],
                                             [w[i][:, k, :] for i in range(2)], h == 0 and k == 0, h == 1 and k == 3)
                            if n == 0 and j == TT - 1 and h == 0:
                                mm.then_inc(op_quarter, 1)
                        if n == 1:
                            mm.then_inc(op_done, 1)
                        if n == 1 and j >= 2:
                            turn(2 * l, j - 2)

            def turn(q, j):
                pe.wait_ge(ln_out, TT * q + j + 1)
                for k in range(KD):
                    mm = pe.transpose(bank[4 * (k // 4) + j][:, P * (k % 4):P * (k % 4) + P],
                                      xtok[:, j, P * k:P * k + P], ident)
                mm.then_inc(tr_done, 1)

            def logits(l):
                pe.wait_ge(tr_low, 2 * TT * (2 * l + 1))
                pe.wait_ge(wr_low, l + 1)
                for k in range(KD):
                    mm = product(bank[0][0:E, :], [wrp[i][:, k, :] for i in range(2)],
                                 [xparts[i][:, k, :] for i in range(2)], k == 0, k == KD - 1)
                mm.then_inc(lgT_done, 1)
                pe.wait_ge(lgT_set, l + 1)
                for j in range(TT):
                    mm = pe.transpose(bank[1][:, E * j:E * j + E], lgT[:, P * j:P * j + P], ident[0:E, 0:E])
                mm.then_inc(lg_done, 1)

            def route(l):
                pe.wait_ge(rt_sel, l + 1)
                for j in range(TT + 1):
                    own = j < TT
                    for i in range(j):
                        mm = pe.matmul(bank[2][:, E * j:E * j + E], onesb[:, :], selb[:, i, :],
                                       start=(i == 0), stop=(not own and i == j - 1))
                    if own:
                        pe.matmul(bank[2][:, E * j:E * j + E], utri[:, :], selb[:, j, :], start=(j == 0), stop=True)
                mm.then_inc(rk_done, 1)
                pe.wait_ge(rt_hot, l + 1)
                for q in range(2 * TT):
                    mm = pe.matmul(bank[3][:, 0:2 * MAXCH], hotA[:, q, :], hotB[:, q, :, :],
                                   start=(q == 0), stop=(q == 2 * TT - 1))
                mm.then_inc(tab_done, 1)

            def turn_gathered(c, l):
                pe.wait_ge(gathered, (c + (l + 1)) * 16)
                for k in range(KD):
                    mm = pe.transpose(bank[2 + k // 4][:, P * (k % 4):P * (k % 4) + P], xg[:, P * k:P * k + P], ident)
                mm.then_inc(xg_turned, 1)

            def chunk(l, c):
                pe.wait_ge(sg_set, c + 1)
                for i in range(HALVES):
                    piece, _, s = halves(i)
                    if i < 2:
                        pe.wait_ge(xgT_low, c * 2 + (2 * l + 1 + i))
                    if i == 2:
                        pe.wait_ge(he_set, c + 1)
                    if i == 4:
                        pe.wait_ge(he_first, c + 1)
                        for k in range(KF):
                            if k == KF // 2:
                                pe.wait_ge(he_set, c + 2)
                            mm = pe.transpose(bank[4][:, P * k:P * k + P], sg[:, P * k:P * k + P], ident)
                        mm.then_inc(he_turned, 1)
                        turn_gathered(c + 1, l)
                        pe.wait_ge(y_set, c + (l + 1))
                        pe.wait_ge(heT_high, c + 1)
                    if i == POOL_HALF:
                        pe.wait_ge(half_low_pool, c + 1)
                    else:
                        pe.wait_ge(half_low, lows_done(c, i))
                    if piece < 2:
                        w = [x[:, :].rearrange("p (k n) -> p k n", k=4) for x in (wh[s], wl[s])]
                        for k in range(4):
                            mm = product(bank[piece][:, :], [xgT[m][:, 4 * (i % 2) + k, :] for m in range(2)],
                                         [w[m][:, k, :] for m in range(2)], i % 2 == 0 and k == 0, i % 2 == 1 and k == 3)
                    else:
                        w = [x[:, :].rearrange("p (k n) -> p k n", k=2) for x in (wh[s], wl[s])]
                        for m, parts in ((0, (0, 1)), (1, (0,))):
                            if i == 4 and m == 1:
                                pe.wait_ge(heT_low, c + 1)
                            for n in range(2):
                                for k in range(2):
                                    for q in parts:
                                        mm = pe.matmul(bank[5 + n][:, :], heT[m][:, 2 * (i % 2) + k, :],
                                                       w[q][:, k, 512 * n:512 * n + 512],
                                                       start=(i == 4 and m == 0 and k == 0 and q == 0),
                                                       stop=(i == 5 and m == 1 and k == 1))
                    mm.then_inc(half_used, 1)

            pe.sem_inc(half_used, SLOTS)
            pe.sem_inc(he_turned, 1)
            for l in range(DEPTH):
                project(l)
                scores(l, 0)
                scores(l, 1)
                scores(l, 2)
                turn_probs(l, 0)
                attend(l, 0)
                turn_probs(l, 1)
                scores(l, 3)
                attend(l, 1)
                spatial(l, 0)
                turn_probs(l, 2)
                attend(l, 2)
                spatial(l, 1)
                turn_probs(l, 3)
                attend(l, 3)
                project_out(l)
                turn(2 * l, 2)
                turn(2 * l, 3)
                logits(l)
                route(l)
                pe.wait_ge(tab_set, l + 1)
                turn_gathered(first_chunk(pe, l, 0), l)
                with pe.Fori(first_chunk(pe, l, 0), first_chunk(pe, l, E)) as c:
                    chunk(l, c)
                if l + 1 < DEPTH:
                    for j in range(TT):
                        turn(2 * l + 1, j)

        @block.scalar
        def _(act):
            def bias(i):
                return col[:, C_BIN + i:C_BIN + i + 1]

            def tile(l, t):
                act.wait_ge(proj_done, PROJ * l + t + 1)
                return bank[t % 4][:, :]

            def piece(l, q):
                n = PIECES * l + q
                act.wait_ge(wraw_in[n % 2], 16 * (n // 2 + 1))
                if q in PIECE_FREE:
                    act.wait_ge(proj_done, PROJ * l + PIECE_FREE[q])
                elif q == PIECES - 1:
                    act.wait_ge(op_quarter, l + 1)
                act.activation(wh[n % SLOTS][:, :], wraw[n % 2], ACT.Copy).then_inc(piece_high, 1)

            def project(l):
                if l == 0:
                    piece(l, 0)
                    for i in range(4):
                        act.wait_ge(xT_in[i], 16)
                        act.activation(xparts[0][:, 2 * i:2 * i + 2, :], xraw[:, 2 * i:2 * i + 2, :], ACT.Copy)\
                           .then_inc(xT_high, 1)
                    piece(l, 1)
                act.wait_ge(col_in, 16 * (l + 1))
                for m in range(2):
                    if l == 0 and m == 1:
                        piece(l, 2)
                    src = tile(l, 2 * m)
                    act.activation(u[:, m, :], src, ACT.Sigmoid, bias=bias(m)).then_inc(sig_set, 1)
                    act.wait_ge(sig_set, 2 * l + m + 1)
                    act.sem_inc(proj_act, 1)
                piece(l, 3)
                for m in range(4):
                    if m == 0:
                        piece(l, 4)
                    if m == 2:
                        piece(l, 5)
                    src = tile(l, 4 + m)
                    act.activation(qr[:, m, :], src, ACT.Identity, bias=bias(4 + m)).then_inc(proj_act, 1)
                piece(l, 6)
                src = tile(l, 8)
                act.activation(kr, src, ACT.Identity, bias=bias(8)).then_inc(proj_act, 1)
                src = tile(l, 9)
                act.activation(vT, src, ACT.Identity, bias=bias(9)).then_inc(proj_act, 1)
                piece(l, 7)
                for m in range(2):
                    src = tile(l, 10 + m)
                    act.activation(gvT[:, m, :], src, ACT.Gelu_apprx_tanh, bias=bias(10 + m)).then_inc(proj_act, 1)
                    if m == 0:
                        conv_squares(l)
                piece(l, 8)
                conv_deviation(l)
                act.wait_ge(glu_read, 2 * (l + 1))
                for m in range(2):
                    src = tile(l, 12 + m)
                    act.activation(u[:, m, :], src, ACT.Gelu_apprx_tanh, bias=bias(12 + m)).then_inc(proj_act, 1)

            def conv_squares(l):
                for m in range(2):
                    act.wait_ge(cen_set, 2 * l + m + 1)
                    act.activation(tmp[:, T * m:T * m + T], cv[:, m, :], ACT.Square).then_inc(sq_set, 1)

            def conv_deviation(l):
                act.wait_ge(var_done, l + 1)
                act.activation(tmp[:, 0:T], bank[7][:, :], ACT.Sqrt, bias=eps).then_inc(sd_set, 1)

            def conv_silu(l):
                for m in range(2):
                    act.wait_ge(conv_norm, 2 * l + m + 1)
                    act.activation(cv[:, m, :], cv[:, m, :], ACT.Silu, bias=col[:, C_CLB + m:C_CLB + m + 1],
                                   scale=col[:, C_CG + m:C_CG + m + 1]).then_inc(conv_raw, 1)

            def conv_split(l):
                act.wait_ge(proj_done, PROJ * (l + 1))
                for m in range(2):
                    act.wait_ge(conv_raw, 2 * l + m + 1)
                    act.activation(xparts[0][:, m, :], cv[:, m, :], ACT.Copy).then_inc(conv_high, 1)

            def gm_split(l, m):
                act.wait_ge(gm_raw, 2 * l + m + 1)
                act.activation(xparts[0][:, 6 + m, :], gmr[:, m, :], ACT.Copy).then_inc(gm_high, 1)

            def softmax(l, b):
                n = TT * l + b
                act.wait_ge(s_max, n + 1)
                if b > 1:
                    act.wait_ge(pt_done, n - 1)
                else:
                    act.wait_ge(conv_norm, 2 * (l + 1))
                act.activation(ses[b % 2], ses[b % 2], ACT.Exp)
                for h in range(NQ):
                    x = act.activation(Pm[b % 2][:, h, :], bank[4 + 2 * (b % 2) + h // 4][:, P * (h % 4):P * (h % 4) + P],
                                       ACT.Exp, bias=snmax[b % 2][:, h:h + 1], scale=HD ** -0.5,
                                       accum_out=ssum[b % 2][:, h:h + 1])
                x.then_inc(p_done, 1)

            def copy_turned(l, b):
                n = TT * l + b
                act.wait_ge(pt_done, n + 1)
                if b > 0:
                    act.wait_ge(o_done, n)
                act.activation(PT[:, 0:4, :], bank[0][:, :].rearrange("p (h q) -> p h q", h=4), ACT.Copy)\
                   .then_inc(pt_act, 1)

            def heads_high(l, b):
                n = TT * l + b
                act.wait_ge(o_done, n + 1)
                act.activation(xparts[0][:, 2:6, P * b:P * b + P].rearrange("p m (c q) -> p m c q", c=2),
                               bank[2][:, :].rearrange("p (c m q) -> p m c q", c=2, m=4), ACT.Copy).then_inc(o_high, 1)

            def columns_high(q, j):
                act.wait_ge(tr_done, TT * q + j + 1)
                for i in range(2):
                    act.activation(xparts[0][:, 4 * i:4 * i + 4, P * j:P * j + P],
                                   bank[4 * i + j][:, :].rearrange("p (k t) -> p k t", k=4), ACT.Copy)\
                       .then_inc(tr_high, 1)

            def scaled(q, j):
                act.wait_ge(ln_rstd, TT * q + j + 1)
                act.wait_ge(ln_norm, TT * q + j + 1)
                act.activation(xtok[:, j, :], xtok[:, j, :], ACT.Copy, scale=rstd[:, j:j + 1]).then_inc(ln_scaled, 1)

            def hidden_high(c, l):
                act.wait_ge(he_turned, c + 2)
                act.activation(heT[0], bank[4][:, :].rearrange("p (k t) -> p k t", k=KF), ACT.Copy)\
                   .then_inc(heT_high, 1)

            def result(c, l, back):
                act.wait_ge(half_used, halves_done(c, 2, back))
                act.wait_ge(cur_set, c + (l + 2 - back))
                act.activation(ysb[:, 0:512], bank[5][:, :], ACT.Copy, scale=gate_cur[:, :])
                act.activation(ysb[:, 512:1024], bank[6][:, :], ACT.Copy, scale=gate_cur[:, :]).then_inc(y_set, 1)

            def half_high_part(c, i, l, pair, r):
                p, cols, s = halves(i)
                if i % 2 == 0:
                    act.wait_ge(wexp_in[r][p], (pair + (l * (E // 2) + 1)) * 16)
                act.wait_ge(half_used, c * HALVES + (i + 1))
                act.activation(wh[s][:, :], slot[r][p][:, cols], ACT.Copy).then_inc(half_high, 1)

            def gathered_high(i):
                act.activation(xgT[0][:, 4 * i:4 * i + 4, :], bank[2 + i][:, :].rearrange("p (k t) -> p k t", k=4),
                               ACT.Copy).then_inc(xgT_high, 1)

            def chunk(l, c, pair, r):
                half_high_part(c, 0, l, pair, r)
                half_high_part(c, 1, l, pair, r)
                result(c, l, 1)
                half_high_part(c, 2, l, pair, r)
                half_high_part(c, 3, l, pair, r)
                half_high_part(c, 4, l, pair, r)
                act.wait_ge(half_used, halves_done(c, 0))
                act.wait_ge(he_turned, c + 1)
                act.activation(sg, bank[0][:, :], ACT.Silu).then_inc(sg_set, 1)
                half_high_part(c, 5, l, pair, r)
                hidden_high(c, l)
                act.wait_ge(xg_turned, c + (l + 2))
                act.wait_ge(half_used, halves_done(c, 1))
                gathered_high(0)
                gathered_high(1)

            act.sem_inc(sg_set, 1)
            for l in range(DEPTH):
                project(l)
                softmax(l, 0)
                softmax(l, 1)
                copy_turned(l, 0)
                piece(l, 9)
                softmax(l, 2)
                heads_high(l, 0)
                copy_turned(l, 1)
                softmax(l, 3)
                heads_high(l, 1)
                conv_silu(l)
                conv_split(l)
                copy_turned(l, 2)
                heads_high(l, 2)
                gm_split(l, 0)
                copy_turned(l, 3)
                gm_split(l, 1)
                heads_high(l, 3)
                piece(l, PIECES - 1)
                scaled(2 * l, 0)
                scaled(2 * l, 1)
                columns_high(2 * l, 0)
                scaled(2 * l, 2)
                act.wait_ge(op_done, TT * (l + 1))
                act.wait_ge(wr_in, 16)
                act.activation(wrp[0], wr[:, :, :], ACT.Copy).then_inc(wr_high, 1)
                for j in range(1, TT):
                    columns_high(2 * l, j)
                act.activation(idle[:, :], eps, ACT.Exp)
                act.wait_ge(lgT_done, l + 1)
                act.activation(lgT, bank[0][0:E, :], ACT.Copy).then_inc(lgT_set, 1)
                act.wait_ge(rt_sub, l + 1)
                act.activation(ex, lg, ACT.Exp).then_inc(rt_exp, 1)
                act.activation(idle[:, :], eps, ACT.Silu)
                act.wait_ge(tab_set, l + 1)
                act.wait_ge(xg_turned, first_chunk(act, l, 0) + (l + 1))
                gathered_high(0)
                gathered_high(1)
                chunk_loops(act, l, lambda c, pair, r: chunk(l, c, pair, r))
                end = first_chunk(act, l, E)
                result(end, l, 1)
                act.wait_ge(scattered, (end + (l + 1)) * 16)
                for j in range(TT):
                    if j >= 2:
                        act.wait_ge(y_added, TT * l + j - 1)
                    act.dma_start(ycomb[j % 2], yd[l].rearrange("(r j p) n -> j p r n", r=2, p=P)[j])\
                       .then_inc(y_in[j % 2], 16)
                    if l + 1 < DEPTH and j == 1:
                        piece(l + 1, 0)
                        piece(l + 1, 1)
                    if j >= 2:
                        scaled(2 * l + 1, j - 2)
                if l + 1 < DEPTH:
                    columns_high(2 * l + 1, 0)
                scaled(2 * l + 1, TT - 2)
                if l + 1 < DEPTH:
                    for j in range(1, TT):
                        columns_high(2 * l + 1, j)
                    piece(l + 1, 2)

        @block.vector
        def _(dve):
            chain = [0]

            def link(x):
                chain[0] += 1
                x.then_inc(dve_chain, 1)
                dve.wait_ge(dve_chain, chain[0])

            def norm_stats(src, j, halves):
                for i, s in enumerate(src):
                    link(dve.bn_stats(bn6[:, 6 * i:6 * i + 6], s))
                link(dve.bn_aggr(mv[:, 2 * j:2 * j + 2], bn6[:, 0:6 * halves]))

            def low(out, src, high):
                return dve.tensor_tensor(out, src, high.bitcast(F32), ALU.subtract)

            def rope(l, n, x):
                dve.wait_ge(rot_done, 5 * l + n + 1)
                dve.wait_ge(mixc_in, 16 * (l + 1))
                link(dve.tensor_tensor(tmp[:, 0:T], bank[4 + n % 4][:, :], sinT, ALU.mult))
                link(dve.tensor_tensor(x, x, cosT, ALU.mult))
                link(dve.tensor_tensor(x, x, tmp[:, 0:T], ALU.add))
                dve.sem_inc(rot_used, 1)

            def gate_conv(l, m):
                dve.wait_ge(proj_done, PROJ * l + 2 * m + 2)
                dve.wait_ge(sig_set, 2 * l + m + 1)
                link(dve.scalar_tensor_tensor(glu[:, m, TAPS - 1:], bank[2 * m + 1][:, :],
                                              col[:, C_BIN + 2 + m:C_BIN + 3 + m], u[:, m, :], ALU.add, ALU.mult))
                dve.sem_inc(proj_dve, 1)
                dve.sem_inc(glu_read, 1)

            def taps(m, lo, hi):
                w = C_CW + TAPS * m
                acc = [cv[:, m, :], tmp[:, T:2 * T]]
                for k in range(lo, hi):
                    x, wk, o = glu[:, m, k:k + T], col[:, w + k:w + k + 1], acc[k % 2]
                    if k == 0:
                        y = dve.tensor_scalar(o, x, wk, col[:, C_CB + m:C_CB + m + 1], ALU.mult, ALU.add)
                    elif k == 1:
                        y = dve.tensor_scalar(o, x, wk, None, ALU.mult)
                    else:
                        y = dve.scalar_tensor_tensor(o, x, wk, o, ALU.mult, ALU.add)
                    chain[0] += 1
                    y.then_inc(dve_chain, 1)
                    dve.wait_ge(dve_chain, chain[0] - 1)
                if hi == TAPS:
                    dve.wait_ge(dve_chain, chain[0])
                    link(dve.tensor_tensor(acc[0], acc[0], acc[1], ALU.add))
                    dve.sem_inc(conv_acc, 1)

            def softmax_max(l, b):
                n = TT * l + b
                i = b % 2
                dve.wait_ge(s_done, n + 1)
                for g in range(2):
                    link(dve.tensor_reduce(smax[i][:, 4 * g:4 * g + 4],
                                           bank[4 + 2 * i + g][:, :].rearrange("p (h k) -> p h k", h=4), AX.X, ALU.max))
                link(dve.scalar_tensor_tensor(smax[i], smax[i], HD ** -0.5, col[:, C_SINK:C_SINK + NQ],
                                              ALU.mult, ALU.max))
                dve.tensor_scalar(snmax[i], smax[i], -1.0, None, ALU.mult)
                link(dve.tensor_tensor(ses[i], col[:, C_SINK:C_SINK + NQ], smax[i], ALU.subtract))
                dve.sem_inc(s_max, 1)

            def softmax_norm(l, b):
                n = TT * l + b
                i = b % 2
                dve.wait_ge(p_done, n + 1)
                link(dve.tensor_tensor(ssum[i], ssum[i], ses[i], ALU.add))
                link(dve.reciprocal(ssum[i], ssum[i]))
                dve.tensor_tensor(Pm[i], Pm[i], ssum[i].unsqueeze(2).broadcast_to([P, NQ, P]), ALU.mult).then_inc(pn_done, 1)

            def copy_turned(l, b):
                n = TT * l + b
                dve.wait_ge(pt_done, n + 1)
                if b > 0:
                    dve.wait_ge(o_done, n)
                dve.tensor_copy(PT[:, 4:8, :], bank[1][:, :].rearrange("p (h q) -> p h q", h=4)).then_inc(pt_dve, 1)

            def gmlp(l, m):
                dve.wait_ge(gm_done, 2 * l + m + 1)
                bc = bsp[:, m, :].unsqueeze(1).broadcast_to([P, TT, P])
                ps = bank[3][:, :].rearrange("p (j i) -> p j i", j=TT)
                link(dve.tensor_tensor(gmr[:, m, :].rearrange("p (j i) -> p j i", j=TT), ps, bc, ALU.add))
                dve.tensor_tensor(gmr[:, m, :], gmr[:, m, :], u[:, m, :], ALU.mult).then_inc(gm_raw, 1)

            def conv_lows(l):
                for m in range(2):
                    dve.wait_ge(conv_high, 2 * l + m + 1)
                    low(xparts[1][:, m, :], cv[:, m, :], xparts[0][:, m, :]).then_inc(conv_low, 1)

            def gm_lows(l, m):
                dve.wait_ge(gm_high, 2 * l + m + 1)
                low(xparts[1][:, 6 + m, :], gmr[:, m, :], xparts[0][:, 6 + m, :]).then_inc(gm_low, 1)

            def heads_low(l, b):
                dve.wait_ge(o_high, TT * l + b + 1)
                h, w = (x[:, 2:6, P * b:P * b + P].rearrange("p m (c q) -> p m c q", c=2) for x in xparts)
                low(w, bank[2][:, :].rearrange("p (c m q) -> p m c q", c=2, m=4), h).then_inc(o_low, 1)

            def columns_low(q, j):
                for i in range(2):
                    dve.wait_ge(tr_high, 2 * (TT * q + j) + i + 1)
                    h, w = (x[:, 4 * i:4 * i + 4, P * j:P * j + P] for x in xparts)
                    low(w, bank[4 * i + j][:, :].rearrange("p (k t) -> p k t", k=4), h).then_inc(tr_low, 1)

            def norm_in(l, j, ffn):
                q = 2 * l + ffn
                if ffn:
                    if j % 2:
                        dve.wait_ge(y_summed, TT // 2 * l + j // 2 + 1)
                    else:
                        dve.wait_ge(y_in[0], 16 * (2 * l + j // 2 + 1))
                    link(dve.scalar_tensor_tensor(xtok[:, j, :], xtok[:, j, :], ALPHA, ycomb[j % 2][:, 0, :],
                                                  ALU.mult, ALU.add))
                    if j % 2 == 0:
                        link(dve.tensor_tensor(xtok[:, j, :], xtok[:, j, :], ycomb[0][:, 1, :], ALU.add))
                    dve.sem_inc(y_added, 1)
                else:
                    dve.wait_ge(xb_done, TT * l + j + 1)
                    dve.wait_ge(op_done, TT * l + j + 1)
                    for n in range(2):
                        x = xtok[:, j, 512 * n:512 * n + 512]
                        link(dve.tensor_tensor(x, x, bank[4 * n + j][:, :], ALU.add))
                norm_stats([xtok[:, j, 0:512], xtok[:, j, 512:1024]], j, 2)
                link(dve.tensor_scalar(ve[:, j:j + 1], mv[:, 2 * j + 1:2 * j + 2], EPS, None, ALU.add))
                dve.sem_inc(ln_var, 1)

            def norm_out(l, j, ffn):
                q = TT * (2 * l + ffn) + j
                dve.wait_ge(ln_rstd, q + 1)
                dve.wait_ge(ln_norm, q + 1)
                dve.wait_ge(ln_out, q)
                dve.scalar_tensor_tensor(xtok[:, j, :], xtok[:, j, :], rstd[:, j:j + 1], rows3[:, 1 if ffn else 2, :],
                                         ALU.mult, ALU.add).then_inc(ln_out, 1)

            def norm(l, ffn):
                dve.wait_ge(rows_in, 32 * l + (32 if ffn else 16))
                for j in range(TT):
                    norm_in(l, j, ffn)
                    dve.scalar_tensor_tensor(xtok[:, j, :], xtok[:, j, :], mv[:, 2 * j:2 * j + 1],
                                             rows3[:, 0 if ffn else 1, :], ALU.subtract, ALU.mult).then_inc(ln_norm, 1)
                    if j == TT - 1:
                        norm_out(l, j, ffn)
                    if j >= 2 and not (ffn and l == DEPTH - 1):
                        columns_low(2 * l + ffn, j - 2)

            def bc3(x, n):
                return x.unsqueeze(2).broadcast_to([P, x.shape[1], n])

            def route(l):
                dve.wait_ge(lg_done, l + 1)
                ps = bank[1][:, 0:TT * E].rearrange("p (j e) -> p j e", j=TT)
                top, tot, s1, s2, m1, m2 = r4
                link(dve.tensor_reduce(top, ps, AX.X, ALU.max))
                link(dve.tensor_tensor(lg, ps, bc3(top, E), ALU.subtract))
                dve.sem_inc(rt_sub, 1)
                dve.wait_ge(rt_exp, l + 1)
                link(dve.tensor_reduce(tot, ex, AX.X, ALU.add))
                link(dve.reciprocal(tot, tot))
                link(dve.tensor_tensor(ex, ex, bc3(tot, E), ALU.mult))
                rb = col[:, C_RB:C_RB + E].unsqueeze(1).broadcast_to([P, TT, E])
                link(dve.tensor_tensor(sel, ex, rb, ALU.add))
                s4 = sel.rearrange("p j (g m) -> p (j g) m", g=G)
                dve.tensor_tensor(pr[:, :, 0:3], s4[:, :, 0:3], s4[:, :, 1:4], ALU.add)
                dve.tensor_tensor(pr[:, :, 3:5], s4[:, :, 0:2], s4[:, :, 2:4], ALU.add)
                link(dve.tensor_tensor(pr[:, :, 5:6], s4[:, :, 0:1], s4[:, :, 3:4], ALU.add))
                link(dve.tensor_reduce(gsc.rearrange("p j g -> p (j g)"), pr, AX.X, ALU.max))

                def first_max(hot, vals, keys, width, m):
                    link(dve.tensor_reduce(m, vals, AX.X, ALU.max))
                    link(dve.tensor_tensor(hot, vals, bc3(m, width), ALU.is_equal))
                    kb = keys.unsqueeze(1).broadcast_to([P, TT, width])
                    link(dve.tensor_tensor(hot, hot, kb, ALU.mult))
                    link(dve.tensor_reduce(m, hot, AX.X, ALU.max))
                    link(dve.tensor_tensor(hot, hot, bc3(m, width), ALU.is_equal))

                first_max(ing, gsc, cst[:, K_KG:K_KG + G], G, m1)
                inb = ing.rearrange("p j g -> p (j g)").unsqueeze(2).broadcast_to([P, TT * G, EG])
                link(dve.tensor_tensor(smk.rearrange("p j (g m) -> p (j g) m", g=G), s4, inb, ALU.mult))
                link(dve.tensor_scalar(gkey, ing, 1e30, -1e30, ALU.mult, ALU.add))
                gb = gkey.rearrange("p j g -> p (j g)").unsqueeze(2).broadcast_to([P, TT * G, EG])
                s4m = smk.rearrange("p j (g m) -> p (j g) m", g=G)
                link(dve.tensor_tensor(s4m, s4m, gb, ALU.add))
                ke = cst[:, K_KE:K_KE + E]
                first_max(oh1, smk, ke, E, m1)
                link(dve.scalar_tensor_tensor(smk, oh1, -3e38, smk, ALU.mult, ALU.add))
                first_max(oh2, smk, ke, E, m2)
                link(dve.tensor_tensor(selb[:, :, :], oh1, oh2, ALU.add))
                dve.sem_inc(rt_sel, 1)

                def pick(out, vals, hot):
                    link(dve.tensor_tensor(kk, vals, hot, ALU.mult))
                    link(dve.tensor_reduce(out, kk, AX.X, ALU.add))

                pick(s1, ex, oh1)
                pick(s2, ex, oh2)
                link(dve.tensor_tensor(m1, s1, s2, ALU.add))
                link(dve.reciprocal(m1, m1))
                dve.tensor_tensor(gt[:, 0:TT], s1, m1, ALU.mult)
                link(dve.tensor_tensor(gt[:, TT:2 * TT], s2, m1, ALU.mult))
                dve.wait_ge(rk_done, l + 1)
                cnt = bank[2][:, TT * E:TT * E + E]
                link(dve.tensor_scalar(nch, cnt, float(P), 1.0, ALU.is_gt, ALU.add))
                for n in (2, 3):
                    link(dve.scalar_tensor_tensor(nch, cnt, float(P * n), nch, ALU.is_gt, ALU.add))
                if l == 0:
                    link(dve.memset(startf[:, 0, 0:1], 0.0))
                else:
                    link(dve.tensor_copy(startf[:, l, 0:1], startf[:, l - 1, E:E + 1]))
                link(dve.memset(zero16, 0.0))
                link(dve.tensor_tensor_scan(startf[:, l, 1:E + 1], nch, zero16, startf[:, l, 0:1], ALU.add, ALU.add))
                rank = bank[2][:, 0:TT * E].rearrange("p (j e) -> p j e", j=TT)
                stb = startf[:, l, 0:E].unsqueeze(1).broadcast_to([P, TT, E])
                for i, hot in enumerate((oh1, oh2)):
                    pick(rk[:, TT * i:TT * i + TT], rank, hot)
                    pick(stc[:, TT * i:TT * i + TT], stb, hot)
                link(dve.tensor_scalar(ovf, rk, float(P), None, ALU.is_ge))
                for n in (2, 3):
                    link(dve.scalar_tensor_tensor(ovf, rk, float(P * n), ovf, ALU.is_ge, ALU.add))
                link(dve.tensor_tensor(stc, stc, ovf, ALU.add))
                link(dve.scalar_tensor_tensor(rk, ovf, -float(P), rk, ALU.mult, ALU.add))
                iota = cst[:, K_IOTA:K_IOTA + P]
                dve.tensor_tensor(hotA, iota.unsqueeze(1).broadcast_to([P, 8, P]), bc3(rk, P), ALU.is_equal)
                link(dve.tensor_tensor(hotB[:, :, 0, :], iota[:, 0:MAXCH].unsqueeze(1).broadcast_to([P, 8, MAXCH]),
                                       bc3(stc, MAXCH), ALU.is_equal))
                link(dve.tensor_tensor(hotB[:, :, 1, :], hotB[:, :, 0, :], bc3(gt, MAXCH), ALU.mult))
                link(dve.tensor_tensor(hotB[:, :, 0, :], hotB[:, :, 0, :], bc3(cst[:, K_DEST:K_DEST + 8], MAXCH),
                                       ALU.mult))
                dve.sem_inc(rt_hot, 1)
                dve.wait_ge(tab_done, l + 1)
                link(dve.tensor_scalar(tabf, bank[3][:, 0:MAXCH], float(OOB), None, ALU.add))
                dve.tensor_copy(gatef[:, :], bank[3][:, MAXCH:2 * MAXCH])
                dve.tensor_copy(dsti[:, :], tabf)
                dve.tensor_copy(starti[:, l * (E + 1):(l + 1) * (E + 1)], startf[:, l, :])
                link(dve.tensor_scalar(tab2, tabf, float(T), -float(T), ALU.is_ge, ALU.mult))
                link(dve.tensor_tensor(toki[:, :], tabf, tab2, ALU.add))
                dve.sem_inc(tab_set, 1)

            def hidden(c, l):
                dve.wait_ge(half_used, halves_done(c, 1))
                dve.wait_ge(sg_set, c + 2)
                dve.tensor_tensor(sg[:, 0:256], bank[1][:, 0:256], sg[:, 0:256], ALU.mult).then_inc(he_first, 1)
                dve.tensor_tensor(sg[:, 256:512], bank[1][:, 256:512], sg[:, 256:512], ALU.mult).then_inc(he_set, 1)
                dve.wait_ge(heT_high, c + 1)
                low(heT[1], bank[4][:, :].rearrange("p (k t) -> p k t", k=KF), heT[0]).then_inc(heT_low, 1)

            def half_low_part(c, i, r):
                p, cols, s = halves(i)
                dve.wait_ge(half_high, c * HALVES + (i + 1))
                low(wl[s][:, :], slot[r][p][:, cols], wh[s][:, :]).then_inc(half_low, 1)
                if i in (1, 3):
                    dve.wait_ge(half_low, lows_done(c, i))
                    dve.sem_inc(split_done[p], 1)

            def gathered_low(c, l, i):
                dve.wait_ge(xgT_high, c * 2 + (2 * l + 1 + i))
                low(xgT[1][:, 4 * i:4 * i + 4, :], bank[2 + i][:, :].rearrange("p (k t) -> p k t", k=4),
                    xgT[0][:, 4 * i:4 * i + 4, :]).then_inc(xgT_low, 1)

            def chunk(l, c, pair, r):
                half_low_part(c, 0, r)
                for i in range(1, HALVES):
                    if i != POOL_HALF:
                        half_low_part(c, i, r)
                hidden(c, l)
                gathered_low(c + 1, l, 0)
                gathered_low(c + 1, l, 1)

            dve.memset(onesc[:, :], 1.0 / CONV).then_inc(ones_set, 1)
            dve.memset(onesb[:, :], 1.0).then_inc(ones_set, 1)
            dve.sem_inc(he_set, 1)
            link(dve.memset(eps, EPS))
            link(dve.memset(mhalf, -0.5))
            dve.wait_ge(piece_high, 1)
            low(wl[0][:, :], wraw[0], wh[0][:, :]).then_inc(piece_low, 1)
            for i in range(4):
                dve.wait_ge(xT_high, i + 1)
                low(xparts[1][:, 2 * i:2 * i + 2, :], xraw[:, 2 * i:2 * i + 2, :], xparts[0][:, 2 * i:2 * i + 2, :])\
                    .then_inc(xT_low, 1)
            for l in range(DEPTH):
                dve.wait_ge(col_in, 16 * (l + 1))
                link(dve.memset(glu[:, :, 0:TAPS - 1], 0.0))
                gate_conv(l, 0)
                taps(0, 0, TAPS)
                gate_conv(l, 1)
                if l == 0:
                    dve.wait_ge(mixc_in, 16)
                    dve.tensor_copy(utri[:, :], mixc[:, M_UTRI:M_UTRI + P]).then_inc(ones_set, 1)
                taps(1, 0, 16)
                for n in range(3):
                    rope(l, n, qr[:, n, :])
                dve.memset(wsT[64:P, :, 0:64], 0.0).then_inc(ws_zeroed, 1)
                taps(1, 16, TAPS)
                rope(l, 3, qr[:, 3, :])
                rope(l, 4, kr)
                dve.wait_ge(mean_done, l + 1)
                for m in range(2):
                    dve.tensor_tensor(cv[:, m, :], cv[:, m, :], bank[6][:, :], ALU.subtract).then_inc(cen_set, 1)
                dve.wait_ge(v_turned, l + 1)
                link(dve.tensor_copy(vmem[:, 0, :, :], bank[5][:, :].rearrange("p (j c) -> p j c", j=TT)))
                dve.sem_inc(v_set, 1)
                for g in range(2):
                    link(dve.memset(bank[4 + g][0:64, :].rearrange("p (h k) -> p h k", h=4)[:, :, 0:64], -1e30))
                dve.sem_inc(mask_set, 1)
                dve.wait_ge(gv_turned, l + 1)
                gsrc = [bank[2 + j // 2][:, GM * (j % 2):GM * (j % 2) + GM] for j in range(TT)]
                for j in range(TT):
                    norm_stats([gsrc[j]], j, 1)
                link(dve.tensor_scalar(ve, mv.rearrange("p (j s) -> p s j", s=2)[:, 1, :], EPS, None, ALU.add))
                dve.sem_inc(gvar_set, 1)
                dve.wait_ge(sd_set, l + 1)
                link(dve.reciprocal(tmp[:, 0:T], tmp[:, 0:T]))
                dve.wait_ge(cen_set, 2 * (l + 1))
                for m in range(2):
                    dve.tensor_tensor(cv[:, m, :], cv[:, m, :], tmp[:, 0:T], ALU.mult).then_inc(conv_norm, 1)
                softmax_max(l, 0)
                softmax_max(l, 1)
                dve.wait_ge(grstd_set, l + 1)
                for j in range(TT):
                    link(dve.tensor_scalar(gv[:, j, :], gsrc[j], mv[:, 2 * j:2 * j + 1], rstd[:, j:j + 1],
                                           ALU.subtract, ALU.mult))
                dve.sem_inc(gvh_set, 1)
                softmax_norm(l, 0)
                softmax_max(l, 2)
                copy_turned(l, 0)
                softmax_norm(l, 1)
                heads_low(l, 0)
                softmax_max(l, 3)
                copy_turned(l, 1)
                softmax_norm(l, 2)
                heads_low(l, 1)
                gmlp(l, 0)
                copy_turned(l, 2)
                softmax_norm(l, 3)
                conv_lows(l)
                heads_low(l, 2)
                gm_lows(l, 0)
                copy_turned(l, 3)
                gmlp(l, 1)
                gm_lows(l, 1)
                heads_low(l, 3)
                dve.wait_ge(piece_high, PIECES * (l + 1))
                n = PIECES * (l + 1) - 1
                low(wl[n % SLOTS][:, :], wraw[n % 2], wh[n % SLOTS][:, :]).then_inc(last_low, 1)
                norm(l, 0)
                dve.wait_ge(wr_high, l + 1)
                low(wrp[1], wr[:, :, :], wrp[0]).then_inc(wr_low, 1)
                for j in range(2, TT):
                    columns_low(2 * l, j)
                route(l)
                for i in range(2):
                    gathered_low(first_chunk(dve, l, 0), l, i)
                chunk_loops(dve, l, lambda c, pair, r: chunk(l, c, pair, r))
                norm(l, 1)
                if l + 1 < DEPTH:
                    for j in range(2, TT):
                        columns_low(2 * l + 1, j)

        @block.gpsimd
        def _(pool):
            chain = [0]

            def link(x):
                chain[0] += 1
                x.then_inc(pool_chain, 1)
                pool.wait_ge(pool_chain, chain[0])

            def piece_lows(l, q):
                n = PIECES * l + q
                pool.wait_ge(piece_high, n + 1)
                pool.tensor_tensor(wl[n % SLOTS][:, :], wraw[n % 2], wh[n % SLOTS][:, :].bitcast(F32), ALU.subtract)\
                    .then_inc(piece_low, 1)

            def sum_choices(l, j):
                pool.wait_ge(y_in[1], 16 * (2 * l + j // 2 + 1))
                y = ycomb[1]
                pool.tensor_tensor(y[:, 0, :], y[:, 0, :], y[:, 1, :], ALU.add).then_inc(y_summed, 1)

            def norm(l, ffn):
                q = 2 * l + ffn
                if ffn:
                    sum_choices(l, 1)
                for j in range(TT):
                    pool.wait_ge(ln_var, TT * q + j + 1)
                    pool.tensor_tensor(rstd[:, j:j + 1], ve[:, j:j + 1], mhalf[:, 0:1], ALU.pow).then_inc(ln_rstd, 1)
                    if ffn and j == 2:
                        sum_choices(l, 3)
                    if j < TT - 1:
                        pool.wait_ge(ln_scaled, (TT - 1) * q + j + 1)
                        pool.tensor_tensor(xtok[:, j, :], xtok[:, j, :], rows3[:, 1 if ffn else 2, :], ALU.add)\
                            .then_inc(ln_out, 1)
                    if not ffn:
                        store(x1d[l], q, j).then_inc(x1_stored, 16)
                    elif l == DEPTH - 1:
                        store(a["out"], q, j).then_inc(out_stored, 16)
                if ffn and l + 1 < DEPTH:
                    for n in range(3):
                        piece_lows(l + 1, n)

            def store(to, q, j):
                pool.wait_ge(ln_out, TT * q + j + 1)
                return pool.dma_start(to[P * j:P * j + P, :], xtok[:, j, :])

            def gather(c, l):
                pool.tensor_copy(gather_idx[:, :], toki[:, bass.ds(c, 1)]).then_inc(idx_set, 1)
                pool.wait_ge(idx_set, c + (l + 1))
                pool.sem_inc(gather_sent, 1)
                pool.indirect_dma_start(xg, None, x1d[l], bass.IndirectOffsetOnAxis(ap=gather_idx[:, :], axis=0),
                                        bounds_check=T - 1, oob_is_err=False).then_inc(gathered, 16)

            def scatter(c, l, back):
                pool.wait_ge(dst_set, c + (l + 2 - back))
                pool.wait_ge(y_set, c + (l + 2 - back))
                pool.sem_inc(scatter_sent, 1)
                pool.indirect_dma_start(yd[l], bass.IndirectOffsetOnAxis(ap=scatter_idx[:, :], axis=0), ysb, None,
                                        bounds_check=2 * T - 1, oob_is_err=False).then_inc(scattered, 16)

            def chunk(l, c, r):
                pool.wait_ge(xg_turned, c + (l + 1))
                pool.wait_ge(gathered, (c + (l + 1)) * 16)
                gather(c + 1, l)
                scatter(c, l, 1)
                p, cols, s = halves(POOL_HALF)
                pool.wait_ge(half_high, c * HALVES + (POOL_HALF + 1))
                pool.tensor_tensor(wl[s][:, :], slot[r][p][:, cols], wh[s][:, :].bitcast(F32), ALU.subtract)\
                    .then_inc(half_low_pool, 1)
                pool.wait_ge(half_low_pool, c + 1)
                pool.wait_ge(half_low, lows_done(c, HALVES - 1))
                pool.sem_inc(split_done[p], 1)
                pool.wait_ge(scattered, (c + (l + 1)) * 16)
                pool.tensor_copy(gate_cur[:, :], gatef[:, bass.ds(c, 1)]).then_inc(cur_set, 1)
                pool.tensor_copy(scatter_idx[:, :], dsti[:, bass.ds(c, 1)]).then_inc(dst_set, 1)

            link(pool.memset(xg, 0.0))
            for l in range(DEPTH):
                if l == 0:
                    pool.wait_ge(piece_low, 1)
                for q in range(1 if l == 0 else 3, 7):
                    piece_lows(l, q)
                pool.wait_ge(v_set, l + 1)
                link(pool.memset(vmem[0:64, 1, 0, :], 0.0))
                pool.dma_start(vmem[64:128, 1, :, :], vmem[0:64, 0, :, :]).then_inc(voff_in, 16)
                pool.dma_start(vmem[0:64, 1, 1:TT, :], vmem[64:128, 0, 0:TT - 1, :]).then_inc(voff_in, 16)
                piece_lows(l, 7)
                pool.wait_ge(gvar_set, l + 1)
                pool.tensor_tensor(rstd, ve, mhalf, ALU.pow).then_inc(grstd_set, 1)
                piece_lows(l, 8)
                pool.wait_ge(gvh_set, l + 1)
                pool.wait_ge(row_in, 16 * (l + 1))
                for i, op in ((0, ALU.mult), (1, ALU.add)):
                    link(pool.tensor_tensor(gv, gv, rowm[:, GM * i:GM * i + GM].unsqueeze(1).broadcast_to([P, TT, GM]), op))
                pool.sem_inc(gvn_set, 1)
                if l == 0:
                    pool.wait_ge(xtok_in, 16)
                for j in range(TT):
                    link(pool.tensor_scalar(xtok[:, j, :], xtok[:, j, :], ALPHA, None, ALU.mult))
                    if j == 0:
                        piece_lows(l, 9)
                pool.wait_ge(rows_in, 32 * l + 16)
                for j in range(TT):
                    pool.tensor_tensor(xtok[:, j, :], xtok[:, j, :], rows3[:, 0, :], ALU.add).then_inc(xb_done, 1)
                norm(l, 0)
                pool.wait_ge(x1_stored, 16 * TT * (l + 1))
                pool.wait_ge(tab_set, l + 1)
                pool.memset(gate_cur[:, :], 1.0).then_inc(cur_set, 1)
                pool.memset(scatter_idx[:, :], OOB).then_inc(dst_set, 1)
                gather(first_chunk(pool, l, 0), l)
                chunk_loops(pool, l, lambda c, pair, r: chunk(l, c, r))
                scatter(first_chunk(pool, l, E), l, 1)
                norm(l, 1)
            pool.wait_ge(out_stored, 16 * TT)


def constants():
    c = np.zeros((P, NCONST), np.float32)
    m = np.zeros((P, NMIX), np.float32)
    p = np.arange(P)
    half = ROPE // 2
    c[:, K_ID:K_ID + P] = np.eye(P)
    c[:, K_IOTA:K_IOTA + P] = p[None, :]
    c[:, K_KE:K_KE + E] = E - np.arange(E)
    c[:, K_KG:K_KG + G] = G - np.arange(G)
    for r in range(2):
        for j in range(TT):
            c[:, K_DEST + TT * r + j] = r * T + P * j + p - OOB
    for g in range(2):
        for i in range(half):
            m[64 * g + i + half, M_PERM + 64 * g + i] = -1.0
            m[64 * g + i, M_PERM + 64 * g + i + half] = 1.0
    m[:, M_UTRI:M_UTRI + P] = p[:, None] < p[None, :]
    freq = np.power(np.float32(THETA), -np.arange(half, dtype=np.float32) / np.float32(half)).astype(np.float32)
    ang = (np.arange(T, dtype=np.float32)[None, :] * freq[:, None]).astype(np.float32)
    m[:, M_COS:M_COS + T] = 1.0
    for g in range(2):
        for i in range(2):
            rows = slice(64 * g + half * i, 64 * g + half * (i + 1))
            m[rows, M_COS:M_COS + T] = np.cos(ang)
            m[rows, M_SIN:M_SIN + T] = np.sin(ang)
    return c, m


def kernel(**inputs):
    from concourse import bacc
    from concourse.bass_utils import run_bass_kernel_spmd

    x = {n: np.asarray(v) for n, v in inputs.items()}
    order = np.arange(NQ).reshape(2, 4).T.reshape(-1)
    qcols = (order[:, None] * HD + np.arange(HD)).reshape(-1)
    o_q, o_k, o_v, o_g = 2 * CONV, 2 * CONV + NQ * HD, 2 * CONV + (NQ + NKV) * HD, 2 * CONV + (NQ + 2 * NKV) * HD
    cols = np.concatenate([np.arange(CONV, 2 * CONV), np.arange(CONV), o_q + qcols, np.arange(o_k, o_g),
                           np.arange(o_g + GM, o_g + 2 * GM), np.arange(o_g, o_g + GM)])
    rows = np.concatenate([np.arange(CONV), CONV + qcols, np.arange(CONV + NQ * HD, D)])
    w_in = np.ascontiguousarray(x["w_in"][:, :, cols])
    b_in = x["b_in"][:, cols]

    def columns(v):
        return v.reshape(DEPTH, -1, P).transpose(0, 2, 1)

    conv_w = x["conv_w"].transpose(0, 2, 1).reshape(DEPTH, 2, P, TAPS).transpose(0, 2, 1, 3).reshape(DEPTH, P, 2 * TAPS)
    percol = np.concatenate([
        columns(b_in), conv_w, columns(x["conv_b"]), columns(x["conv_ln_g"]), columns(x["conv_ln_b"]),
        np.broadcast_to(x["attn_sinks"][:, None, :], (DEPTH, P, NQ)),
        np.broadcast_to(x["router_bias"][None, None, :], (DEPTH, P, E))], axis=2)
    const, mixc = constants()
    arrays = {
        "x": x["x"].reshape(T, D), "x_t": np.ascontiguousarray(x["x"].reshape(T, D).T),
        "w_in": w_in, "w_out": np.ascontiguousarray(x["w_out"][:, rows, :]), "cols": np.ascontiguousarray(percol),
        "rowm": np.concatenate([x["gmlp_ln_g"], x["gmlp_ln_b"]], axis=1),
        "ws_t": np.ascontiguousarray(x["gmlp_w_s"].transpose(0, 1, 3, 2)), "gmlp_b_s": x["gmlp_b_s"],
        "rows_mix": np.stack([x["b_out"], x["ln_mix_g"], x["ln_mix_b"]], axis=1),
        "rows_ffn": np.stack([x["ln_ffn_g"], x["ln_ffn_b"]], axis=1),
        "w_router": x["w_router"], "const": const, "mixc": mixc,
        "exp_w_gate": x["exp_w_gate"].reshape(DEPTH * E, D, FE), "exp_w_up": x["exp_w_up"].reshape(DEPTH * E, D, FE),
        "exp_w_down": x["exp_w_down"].reshape(DEPTH * E, FE, D),
    }
    nc = bacc.Bacc("TRN2", target_bir_lowering=False, num_devices=1)
    a = {n: nc.dram_tensor(f"in_{n}", v.shape, mybir.dt.from_np(v.dtype), kind="ExternalInput").ap()
         for n, v in arrays.items()}
    a["out"] = nc.dram_tensor("out_x", (T, D), F32, kind="ExternalOutput").ap()
    build(nc, a)
    r = run_bass_kernel_spmd(nc, [{f"in_{n}": v for n, v in arrays.items()}], core_ids=[0])
    return r.results[0]["out_x"].reshape(1, T, D)
```
